# Optimizing a Trainium2 kernel written in Bass

```python
import jax, jax.numpy as jnp
from jax import lax
import numpy as np

D_MODEL = 2048
BATCH = 1
SEQ = 256
DEPTH = 1
DEC_BATCH = 8
DEC_SEQ = 8
PAST_LEN = 2048
PAGE_SIZE = 128

HEAD_DIM = 128
CONV_WIDTH = (D_MODEL * 3) // 8
POOL_WIDTH = D_MODEL // 4
CHUNK_WIDTH = D_MODEL - CONV_WIDTH - POOL_WIDTH
CONV_K = 3
CHUNK = 128
N_CHUNK_HEADS = CHUNK_WIDTH // HEAD_DIM
POOL_WINDOWS = (2, 4, 8, 16)
N_POOL_GROUPS = len(POOL_WINDOWS)
POOL_GROUP_DIM = POOL_WIDTH // N_POOL_GROUPS
POOL_BUF = max(POOL_WINDOWS) - 1
IN_WIDTH = 3 * CONV_WIDTH + 2 * CHUNK_WIDTH + POOL_WIDTH
N_EXPERT_GROUPS = 4
EXPERTS_PER_GROUP = 4
N_EXPERTS = N_EXPERT_GROUPS * EXPERTS_PER_GROUP
TOP_K_EXPERT = 2
D_EXPERT = D_MODEL // 4
ALPHA = (2 * DEPTH) ** 0.25
BETA = (8 * DEPTH) ** -0.25
LN_EPS = 1e-5

kernel_name = "hybrid_conv_chunkmlp_pool_hmoe_step"

def layer_norm(x, g, b):
    xf = x.astype(jnp.float32)
    mu = jnp.mean(xf, axis=-1, keepdims=True)
    var = jnp.mean(jnp.square(xf - mu), axis=-1, keepdims=True)
    y = (xf - mu) * lax.rsqrt(var + LN_EPS) * g.astype(jnp.float32) + b.astype(jnp.float32)
    return y.astype(x.dtype)

def short_conv(z, buf, w):
    T = z.shape[1]
    ext = jnp.concatenate([buf.astype(z.dtype), z], axis=1)
    y = w[0] * ext[:, 0:T]
    for k in range(1, CONV_K):
        y = y + w[k] * ext[:, k:k + T]
    return y, ext[:, T:]

def chunk_mix(vn, w_s, b_s):
    B, T, _ = vn.shape
    L = min(T, CHUNK)
    nc = T // L
    vc = vn.reshape(B, nc, L, N_CHUNK_HEADS, HEAD_DIM)
    ws = jnp.tril(w_s[:, :L, :L])
    mixed = jnp.einsum('hts,bcshd->bcthd', ws, vc) + jnp.transpose(b_s[:, :L])[None, None, :, :, None]
    return mixed.reshape(B, T, CHUNK_WIDTH)

def multiscale_pool(p, buf, pos0, pool_w, pool_scale):
    B, T, _ = p.shape
    ext = jnp.concatenate([buf.astype(p.dtype), p], axis=1)
    new_buf = ext[:, T:]
    extf = ext.astype(jnp.float32).reshape(B, POOL_BUF + T, N_POOL_GROUPS, POOL_GROUP_DIM)
    cs = jnp.concatenate([jnp.zeros((B, 1, N_POOL_GROUPS, POOL_GROUP_DIM), jnp.float32),
                          jnp.cumsum(extf, axis=1)], axis=1)
    end = cs[:, POOL_BUF + 1:]
    pos = pos0 + jnp.arange(T)
    means = []
    for g, w in enumerate(POOL_WINDOWS):
        start = cs[:, POOL_BUF + 1 - w:POOL_BUF + 1 - w + T, g]
        cnt = jnp.minimum(w, pos + 1).astype(jnp.float32)[None, :, None]
        means.append((end[:, :, g] - start) / cnt)
    pooled = jnp.stack(means, axis=2)
    diff = (pooled - extf[:, POOL_BUF:]).astype(p.dtype)
    y = jnp.einsum('btgc,gcd->btgd', diff, pool_w).reshape(B, T, POOL_WIDTH) * pool_scale
    return y, new_buf

def token_mixer(x, conv_buf, pool_buf, pos0, w_in, conv_w, sgu_ln_g, sgu_ln_b, sgu_w, sgu_b,
                pool_w, pool_scale, w_out):
    h = jnp.einsum('btd,de->bte', x, w_in)
    cuts = [CONV_WIDTH, 2 * CONV_WIDTH, 3 * CONV_WIDTH, 3 * CONV_WIDTH + CHUNK_WIDTH,
            3 * CONV_WIDTH + 2 * CHUNK_WIDTH]
    b_gate, c_gate, h_conv, u, v, p = jnp.split(h, cuts, axis=-1)
    conv_out, new_conv = short_conv(c_gate * h_conv, conv_buf, conv_w)
    y_conv = b_gate * conv_out
    vn = layer_norm(v, sgu_ln_g, sgu_ln_b)
    y_chunk = u * chunk_mix(vn, sgu_w, sgu_b)
    y_pool, new_pool = multiscale_pool(p, pool_buf, pos0, pool_w, pool_scale)
    y = jnp.concatenate([y_conv, y_chunk, y_pool], axis=-1)
    return jnp.einsum('bte,ed->btd', y, w_out), new_conv, new_pool, vn

def hier_moe(x, rg_w, rg_b, re_w, re_b, w_gate, w_up, w_down):
    B, T, D = x.shape
    xt = x.reshape(B * T, D)
    g_logits = (xt @ rg_w).astype(jnp.float32) + rg_b.astype(jnp.float32)
    g_prob = jax.nn.softmax(g_logits, axis=-1)
    g_val, g_idx = lax.top_k(g_prob, 1)
    e_logits = ((xt @ re_w).astype(jnp.float32) + re_b.astype(jnp.float32)).reshape(
        -1, N_EXPERT_GROUPS, EXPERTS_PER_GROUP)
    e_sel = jnp.take_along_axis(e_logits, g_idx[:, :, None], axis=1)[:, 0]
    e_prob = jax.nn.softmax(e_sel, axis=-1)
    e_val, e_idx = lax.top_k(e_prob, TOP_K_EXPERT)
    e_val = e_val / jnp.sum(e_val, axis=-1, keepdims=True)
    gates = g_val * e_val
    ids = g_idx * EXPERTS_PER_GROUP + e_idx
    combine = jnp.sum(jax.nn.one_hot(ids, N_EXPERTS, dtype=jnp.float32) * gates[..., None], axis=1)
    hg = jnp.einsum('nd,edf->nef', xt, w_gate)
    hu = jnp.einsum('nd,edf->nef', xt, w_up)
    a = jax.nn.silu(hg) * hu * combine[:, :, None].astype(x.dtype)
    out = jnp.einsum('nef,efd->nd', a, w_down)
    return out.reshape(B, T, D)

def trunk_layer(x, conv_buf, pool_buf, pos0, w_in, conv_w, sgu_ln_g, sgu_ln_b, sgu_w, sgu_b,
                pool_w, pool_scale, w_out, ln1_g, ln1_b, rg_w, rg_b, re_w, re_b,
                w_gate, w_up, w_down, ln2_g, ln2_b):
    mix, new_conv, new_pool, vn = token_mixer(x, conv_buf, pool_buf, pos0, w_in, conv_w, sgu_ln_g,
                                              sgu_ln_b, sgu_w, sgu_b, pool_w, pool_scale, w_out)
    x = layer_norm(ALPHA * x + mix, ln1_g, ln1_b)
    x = layer_norm(ALPHA * x + hier_moe(x, rg_w, rg_b, re_w, re_b, w_gate, w_up, w_down), ln2_g, ln2_b)
    return x, new_conv, new_pool, vn

def setup_inputs(seed: int = 0) -> dict:
    key = jax.random.key(seed)
    ks = jax.random.split(key, 26)
    f = jnp.float32
    nrm = lambda k, s: jax.random.normal(k, s, f)
    return {
        "x_prompt": nrm(ks[0], (BATCH, SEQ, D_MODEL)),
        "x_sample": nrm(ks[1], (DEC_BATCH, DEC_SEQ, D_MODEL)),
        "state_conv": nrm(ks[2], (DEPTH, DEC_BATCH, CONV_K - 1, CONV_WIDTH)),
        "state_pool": nrm(ks[3], (DEPTH, DEC_BATCH, POOL_BUF, POOL_WIDTH)),
        "w_in": nrm(ks[4], (DEPTH, D_MODEL, IN_WIDTH)) * D_MODEL ** -0.5,
        "conv_w": nrm(ks[5], (DEPTH, CONV_K, CONV_WIDTH)) * CONV_K ** -0.5,
        "sgu_ln_g": 1.0 + 0.1 * nrm(ks[6], (DEPTH, CHUNK_WIDTH)),
        "sgu_ln_b": 0.01 * nrm(ks[7], (DEPTH, CHUNK_WIDTH)),
        "sgu_w": nrm(ks[8], (DEPTH, N_CHUNK_HEADS, CHUNK, CHUNK)) * CHUNK ** -0.5,
        "sgu_b": 1.0 + 0.1 * nrm(ks[9], (DEPTH, N_CHUNK_HEADS, CHUNK)),
        "pool_w": nrm(ks[10], (DEPTH, N_POOL_GROUPS, POOL_GROUP_DIM, POOL_GROUP_DIM)) * POOL_GROUP_DIM ** -0.5,
        "pool_scale": 1.0 + 0.1 * nrm(ks[11], (DEPTH, POOL_WIDTH)),
        "w_out": nrm(ks[12], (DEPTH, D_MODEL, D_MODEL)) * (D_MODEL ** -0.5 * BETA),
        "ln1_g": 1.0 + 0.1 * nrm(ks[13], (DEPTH, D_MODEL)),
        "ln1_b": 0.01 * nrm(ks[14], (DEPTH, D_MODEL)),
        "router_group_w": nrm(ks[15], (DEPTH, D_MODEL, N_EXPERT_GROUPS)) * D_MODEL ** -0.5,
        "router_group_b": 0.01 * nrm(ks[16], (DEPTH, N_EXPERT_GROUPS)),
        "router_expert_w": nrm(ks[17], (DEPTH, D_MODEL, N_EXPERTS)) * D_MODEL ** -0.5,
        "router_expert_b": 0.01 * nrm(ks[18], (DEPTH, N_EXPERTS)),
        "expert_w_gate": nrm(ks[19], (DEPTH, N_EXPERTS, D_MODEL, D_EXPERT)) * D_MODEL ** -0.5,
        "expert_w_up": nrm(ks[20], (DEPTH, N_EXPERTS, D_MODEL, D_EXPERT)) * D_MODEL ** -0.5,
        "expert_w_down": nrm(ks[21], (DEPTH, N_EXPERTS, D_EXPERT, D_MODEL)) * (D_EXPERT ** -0.5 * BETA),
        "ln2_g": 1.0 + 0.1 * nrm(ks[22], (DEPTH, D_MODEL)),
        "ln2_b": 0.01 * nrm(ks[23], (DEPTH, D_MODEL)),
    }

def reference(x_prompt, x_sample, state_conv, state_pool, w_in, conv_w, sgu_ln_g, sgu_ln_b, sgu_w,
              sgu_b, pool_w, pool_scale, w_out, ln1_g, ln1_b, router_group_w, router_group_b,
              router_expert_w, router_expert_b, expert_w_gate, expert_w_up, expert_w_down,
              ln2_g, ln2_b):
    bp = x_prompt.shape[0]
    zero_conv = jnp.zeros((bp, CONV_K - 1, CONV_WIDTH), x_prompt.dtype)
    zero_pool = jnp.zeros((bp, POOL_BUF, POOL_WIDTH), x_prompt.dtype)
    yp, ys = x_prompt, x_sample
    conv_p, pool_p, conv_s, pool_s, v_s = [], [], [], [], []
    for l in range(DEPTH):
        params = (w_in[l], conv_w[l], sgu_ln_g[l], sgu_ln_b[l], sgu_w[l], sgu_b[l], pool_w[l],
                  pool_scale[l], w_out[l], ln1_g[l], ln1_b[l], router_group_w[l], router_group_b[l],
                  router_expert_w[l], router_expert_b[l], expert_w_gate[l], expert_w_up[l],
                  expert_w_down[l], ln2_g[l], ln2_b[l])
        yp, cp, pp, _vp = trunk_layer(yp, zero_conv, zero_pool, 0, *params)
        ys, cs_, ps_, vs_ = trunk_layer(ys, state_conv[l], state_pool[l], PAST_LEN, *params)
        conv_p.append(cp)
        pool_p.append(pp)
        conv_s.append(cs_)
        pool_s.append(ps_)
        v_s.append(vs_)
    new_conv_prompt = jnp.stack(conv_p, axis=0)
    new_pool_prompt = jnp.stack(pool_p, axis=0)
    new_conv_sample = jnp.stack(conv_s, axis=0)
    new_pool_sample = jnp.stack(pool_s, axis=0)
    new_chunk_v_sample = jnp.stack(v_s, axis=0)
    return (yp, ys, new_conv_prompt, new_pool_prompt, new_conv_sample, new_pool_sample, new_chunk_v_sample)


_drawn_inputs = setup_inputs


def setup_inputs(seed=0):
    import zlib

    import numpy as np

    out = dict(_drawn_inputs(seed))
    spreads = {}
    factors = {'sgu_ln_b': 5.804,
     'ln1_b': 3.563,
     'router_group_b': 8.0,
     'router_expert_b': 14.886,
     'ln2_b': 5.779}
    for name, (base, spread) in spreads.items():
        noise = np.random.default_rng([zlib.crc32(name.encode()), seed]).standard_normal(out[name].shape)
        drawn = base * np.exp(spread * noise) if base else spread * noise
        out[name] = __import__('jax').numpy.asarray(drawn.astype(out[name].dtype))
    for name, factor in factors.items():
        out[name] = (out[name] * factor).astype(out[name].dtype)
    return out
```

```python
import concourse.bass as bass
from concourse import mybir

FP32 = mybir.dt.float32
F32R = mybir.dt.float32r
INT32 = mybir.dt.int32
ALU = mybir.AluOpType
ACT = mybir.ActivationFunctionType
AXX = mybir.AxisListType.X

P = 128
ALPHA = 2 ** 0.25
EPS = 1e-5


class Tally:

    def __init__(self, sem):
        self.sem, self.value, self.base, self.per = sem, 0, 0, None

    def inc(self, instruction):
        instruction.then_inc(self.sem, 1)
        self.value = self.value + 1
        self.base += 1
        return self.value

    def enter(self, turn, per):
        self.start, self.per = self.base, per
        self.value = self.base + turn * per

    def leave(self, turns):
        assert self.base - self.start == self.per, (self.base - self.start, self.per)
        self.base = self.value = self.start + self.per * turns


def hybrid_trunk_kernel(nc, x_prompt, x_sample, state_conv, state_pool, w_in, conv_w, sgu_ln_g,
                        sgu_ln_b, sgu_w, sgu_b, pool_w, pool_scale, w_out, ln1_g, ln1_b,
                        rg_w, rg_b, re_w, re_b, w_gate, w_up, w_down, ln2_g, ln2_b,
                        y_prompt, y_sample, new_conv_prompt, new_pool_prompt, new_conv_sample,
                        new_pool_sample, new_chunk_v):
    D = x_prompt.shape[2]
    SEQ = x_prompt.shape[1]
    NB, NT = x_sample.shape[0:2]
    NTOK = SEQ + NB * NT
    TILES = [(0, P), (P, P), (SEQ, NTOK - SEQ)]
    KT = D // P
    CONV = state_conv.shape[3]
    POOL = state_pool.shape[3]
    CHW = D - CONV - POOL
    CT, HT, PT = CONV // P, CHW // P, POOL // P
    PBUF = state_pool.shape[2]
    WINDOWS = (2, 4, 8, 16)
    NG, NE = rg_w.shape[2], re_w.shape[2]
    EG = NE // NG
    F = w_gate.shape[3]
    FT = F // P

    GW = 2 * P
    CK = 8
    CH = CK * GW
    RING = 3
    G_P, G_V, G_U, G_H, G_C, G_B, G_O = 0, 2, 5, 8, 11, 14, 17
    G_END = G_O + D // GW
    CHUNKS1 = 2 * G_END
    TB0 = 6

    uses = [f"x{i}{q}" for i in range(3) for q in range(4)]
    uses += ["par", "spool", "sconv"]
    uses += [f"pool{g}" for g in range(PT)] + ["pout0", "pout1", "ws0", "ws1", "wsb"]
    uses += [f"v{i}{q}" for i in range(3) for q in range(2)]
    uses += [f"mix{h}" for h in range(HT)] + ["z0", "z1"]
    USE = {name: n for n, name in enumerate(uses)}
    USE_O = len(uses)
    USE_R = USE_O + 2 * (G_END - G_O)
    uses = [f"{what}{i}{q}" for i in range(3) for what, q in
            [("r", 0), ("r", 1), ("r", 2), ("r", 3), ("lg", "")]] + ["pos"]
    USE.update({name: USE_R + n for n, name in enumerate(uses)})
    USE_E = USE_R + len(uses)

    C = P
    ROUNDS = -(-NTOK // C)
    STEPS = ROUNDS * NE
    ECH = 12
    LEAD = 3
    BIG = 4096.0

    KB = 1024
    base = (nc.sbuf_base + 63) // 64 * 64

    def at(name, offset, shape, dt=FP32):
        return nc.alloc_sbuf_tensor_at(name, shape, dt, offset=base + offset, align_bytes=4)

    RAW0 = 0
    RING_HI = RAW0 + 6 * 8 * KB
    RING_LO = RING_HI + 24 * KB
    TOK0 = RING_LO + 24 * KB
    XA = TOK0 + 24 * KB
    XT_B = KT * NTOK * 4
    YT_HI0, YT_LO0 = XA + 2 * XT_B, XA + 3 * XT_B
    MISC = XA + 4 * XT_B
    raw = [at(f"raw{s}", RAW0 + s * 8 * KB, [P, CH]) for s in range(6)]
    w_hi = [at(f"w_hi{s}", RING_HI + s * 8 * KB, [P, CH], F32R) for s in range(RING)]
    w_lo = [at(f"w_lo{s}", RING_LO + s * 8 * KB, [P, CH], F32R) for s in range(RING)]
    tok = at("tok", TOK0, [P, 3, D])
    brow = at("brow", TOK0, [P, 3, D])[64:65, 2, 0:HT * P].rearrange("p (h c) -> p h c", h=HT)
    xT_hi = at("xT_hi", XA, [P, KT, NTOK], F32R)
    xT_lo = at("xT_lo", XA + XT_B, [P, KT, NTOK], F32R)
    yT_hi = at("yT_hi", YT_HI0, [P, KT, NTOK], F32R)
    yT_lo = at("yT_lo", YT_LO0, [P, KT, NTOK], F32R)
    ROW = NTOK * 4
    T0 = RAW0 + 24 * KB
    ZW = 2 + SEQ + NB * (2 + NT)
    PW = PBUF + SEQ + NB * (PBUF + NT)
    zext = at("zext", T0, [P, CT, ZW])
    convt = at("convt", T0 + CT * ZW * 4, [P, CT, NTOK])
    PX0 = T0 + CT * ZW * 4 + CT * ROW
    pext = at("pext", PX0, [P, PT, PW])
    PX1 = PX0 + PT * PW * 4
    zstate = at("zstate", PX1, [P, CT, 2 * NB])
    zlast = at("zlast", PX1 + CT * 2 * NB * 4, [P, CT, 2 + 2 * NB])
    sum_a = at("sum_a", T0, [P, PT, PW])
    sum_b = at("sum_b", T0 + PT * PW * 4, [P, PT, PW])
    vtok = at("vtok", T0, [P, 3, CHW])
    wsT = at("wsT", PX0, [P, HT, P])
    wsbT = at("wsbT", PX0 + HT * P * 4, [64, HT, 64])
    p_out = at("p_out", T0 + 9216, [16, PT * P])
    ws_nat = at("ws_nat", YT_HI0, [P, HT, P])
    wsb_nat = at("wsb_nat", YT_HI0 + HT * P * 4, [64, HT, 64])
    sconv_nat = at("sconv_nat", YT_HI0 + HT * (P + 64) * 4, [2 * NB, CONV])
    spool_nat = at("spool_nat", YT_HI0 + 12 * ROW, [NB * PBUF, POOL])
    poolw = at("poolw", YT_HI0 + 12 * ROW + POOL * 4, [P, PT, P])
    vT = at("vT", YT_HI0 + 6 * ROW, [P, HT, NTOK])
    pdiff = at("pdiff", YT_LO0, [P, PT, NTOK])
    pnew = at("pnew", YT_LO0 + 4 * ROW, [P, PT, NB * NT])
    mixu = at("mixu", YT_LO0, [P, HT, NTOK])
    sg_g = at("sg_g", YT_LO0 + 6 * ROW, [P, CHW])
    sg_b = at("sg_b", YT_LO0 + 6 * ROW + CHW * 4, [P, CHW])
    z_out = at("z_out", PX0, [2 + 2 * NB, CONV])
    p_out2 = at("p_out2", T0 + 9216 + PT * P * 4, [64, PT * P])
    par_nat = at("par_nat", PX1 + CT * (2 * NB + 2 + 2 * NB) * 4, [3 * CT + PT, P])
    lng = at("lng", XA, [P, D])
    lnb = at("lnb", XA + 8 * KB, [P, D])
    mixT = [at(f"mixT{s}", XA + 16 * KB + s * 2 * ROW, [P, 2, NTOK]) for s in range(3)]
    tmp = at("tmp", MISC, [P, PT, NTOK])
    CO = MISC + PT * ROW
    ident = at("ident", CO, [P, P])
    before = at("before", CO + 512, [P, P])
    ones = at("ones", CO + 1024, [P, P])
    slots = at("slots", CO + 1536, [P, P])
    parT = at("parT", CO + 2048, [P, 3 * CT + PT])
    rcount = at("rcount", CO + 2144, [P, 16])
    vstats = at("vstats", CO + 2208, [P, 3, 2, 6])
    vmv = at("vmv", CO + 2352, [P, 3, 2])
    vstd = at("vstd", CO + 2376, [P, 3])
    vrstd = at("vrstd", CO + 2388, [P, 3])
    rcount_i = at("rcount_i", CO + 2400, [P, 16], INT32)
    slots_i = at("slots_i", CO + 1536, [P, P], INT32)
    xstats = at("xstats", MISC, [P, 3, 8, 6])
    rg_nat = at("rg_nat", XA + 24064, [P, KT, NG])
    re_nat = at("re_nat", XA + 24320, [P, KT, NE])
    rw = at("rw", XA + 25344, [P, KT, NG + NE])
    rbias = at("rbias", XA + 26624, [1, NG + NE])
    x1T = at("x1T", XA + 26720, [P, KT, NTOK])
    yout = at("yout", XA + 16 * KB, [P, D])
    onehot = at("onehot", XA + 47232, [P, 3, C])
    xg = at("xg", XA + 48 * KB, [P, D])
    xgT_hi = at("xgT_hi", XA + 56 * KB, [P, KT, C], F32R)
    xgT_lo = at("xgT_lo", XA + 64 * KB, [P, KT, C], F32R)
    aT_hi = at("aT_hi", XA + 72 * KB, [P, FT, C], F32R)
    aT_lo = at("aT_lo", XA + 74 * KB, [P, FT, C], F32R)
    silu = at("silu", XA + 76 * KB, [P, F])
    a_sb = at("a_sb", XA + 78 * KB, [P, F])
    yrows = [at(f"yrows{i}", RAW0 + 16 * KB * i, [P, 2, D]) for i in range(3)]
    small = [MISC + 576]

    def little(name, shape, dt=FP32):
        n = 4
        for d in shape[1:]:
            n *= d
        t = at(name, small[0], shape, dt)
        small[0] += n
        assert small[0] <= CO
        return t

    logits = little("logits", [P, 3, NG + NE])
    rank = little("rank", [P, 3, STEPS])
    facts = little("facts", [P, 3, NE, 3])
    token_i = little("token_i", [P, 3], INT32)
    token = little("token", [P, 3])
    first_w = little("first_w", [P, EG])
    first_i = little("first_i", [P, EG], INT32)
    r4 = [little(f"r4_{n}", [P, 3, 4]) for n in range(6)]
    r1 = [little(f"r1_{n}", [P, 3, 1]) for n in range(8)]
    r16 = [little(f"r16_{n}", [P, 3, NE]) for n in range(4)]
    gather_row = little("gather_row", [P, 1], INT32)
    result_rows = little("result_rows", [P, STEPS], INT32)
    result_row = little("result_row", [P, 1], INT32)
    gates = little("gates", [P, STEPS])
    fullest = little("fullest", [P, 2], INT32)
    ps = nc.alloc_psum_tensor("ps", [P, 8, 512], FP32)

    S = nc.alloc_semaphore
    act_step = S("act_step")
    raw_full = [S(f"raw_full{s}") for s in range(6)]
    hi_ready, lo_ready = S("hi_ready"), S("lo_ready")
    w_used = S("w_used")
    x_in = [S(f"x_in{i}") for i in range(3)]
    pool_const = S("pool_const")
    par_in = S("par_in")
    sgu_in = S("sgu_in")
    state_in = S("state_in")
    tb_full = [S(f"tb_full{b}") for b in range(2)]
    tb_free = [S(f"tb_free{b}") for b in range(2)]
    xhi_ready = S("xhi_ready")
    pair_free = [S(f"pair_free{k}") for k in range(3)]
    dve_step = S("dve_step")
    yhi_ready, ylo_ready = S("yhi_ready"), S("ylo_ready")
    diff_ready, z_ready = S("diff_ready"), S("z_ready")
    var_ready, std_ready, vn_ready = S("var_ready"), S("std_ready"), S("vn_ready")
    gb_in = S("gb_in")
    small_out = S("small_out")
    copy_out = S("copy_out")
    sp_turns, pool_turns = S("sp_turns"), S("pool_turns")
    rw_in = S("rw_in")
    rw_ready = S("rw_ready")
    x1_ready, x1_stored = S("x1_ready"), S("x1_stored")
    gexp_in, gexp_out = S("gexp_in"), S("gexp_out")
    mask_ready, facts_ready = S("mask_ready"), S("facts_ready")
    onehot_ready = S("onehot_ready")
    slots_made, rows_ready = S("slots_made"), S("rows_ready")
    xg_zero = S("xg_zero")
    gathered, scattered = S("gathered"), S("scattered")
    silu_ready, a_ready = S("silu_ready"), S("a_ready")
    aT_full, aT_hi_ready, aT_lo_ready = S("aT_full"), S("aT_hi_ready"), S("aT_lo_ready")
    xg_hi_ready = S("xg_hi_ready")
    y_read, yout_free = S("y_read"), S("yout_free")
    result_row_ready = S("result_row_ready")
    experts_done = S("experts_done")
    fin_in = [S(f"fin_in{i}") for i in range(3)]
    ln2_in = S("ln2_in")
    fin_step, fin_sum, fin_std, fin_ready = S("fin_step"), S("fin_sum"), S("fin_std"), S("fin_ready")
    y_out = S("y_out")
    x1_dram = nc.dram_tensor("x1_rows", (NTOK, D), FP32).ap()
    y_dram = nc.dram_tensor("result_rows_dram", (2 * NTOK, D), FP32).ap()

    def tb(n):
        return n % 2, n // 2 + 1

    def wait_read(eng, *names):
        for name in names:
            b, full = tb(USE[name])
            eng.wait_ge(tb_free[b], full)

    def wait_group_read(eng, g):
        eng.wait_ge(pair_free[g % 3], g // 3 + 1)


    win_v = w_in[0].rearrange("(p t) n -> p t n", t=KT)
    wout_v = w_out[0].rearrange("(j p) n -> p j n", p=P)
    COL_P, COL_V = 3 * CONV + 2 * CHW, 3 * CONV + CHW
    x_tiles = [x_prompt[0, 0:P, :], x_prompt[0, P:SEQ, :], x_sample.rearrange("b t d -> (b t) d")]

    HALF_O = (1, 0)

    def wait_alone(eng, sem, value, turns):
        eng.wait_ge(sem, value)
        eng.sem_inc(turns, 1)

    def sp_program(sp):
        for i in range(3):
            m = TILES[i][1]
            sp.dma_start(tok[0:m, i, :], x_tiles[i]).then_inc(x_in[i], 16)
        for c in range(4):
            if c >= RING:
                sp.wait_ge(lo_ready, c - RING + 1)
            g, h = c // 2, c % 2
            sp.dma_start(raw[c % 3][:, :].rearrange("p (t n) -> p t n", t=CK),
                         win_v[:, CK * h:CK * h + CK, COL_P + GW * g:COL_P + GW * (g + 1)])\
              .then_inc(raw_full[c % 3], 16)
        with sp.Fori(0, 5) as s:
            for i in range(6):
                c = 2 * G_V + 6 * s + i
                wait_alone(sp, lo_ready, c - RING + 1, sp_turns)
                k = (2 * G_V + i) % 3
                col = COL_V - CONV * s + GW * (i // 2)
                sp.dma_start(raw[k][:, :].rearrange("p (t n) -> p t n", t=CK),
                             win_v[:, CK * (i % 2):CK * (i % 2) + CK, bass.ds(col, GW)])\
                  .then_inc(raw_full[k], 16)

        def out_chunk(c, k, h, col):
            wait_alone(sp, lo_ready, c - RING + 1, sp_turns)
            sp.dma_start(raw[k][:, :].rearrange("p (t n) -> p t n", t=CK),
                         wout_v[:, CK * h:CK * h + CK, col]).then_inc(raw_full[k], 16)

        with sp.Fori(0, 2) as s:
            for i in range(6):
                out_chunk(2 * G_O + 6 * s + i, (2 * G_O + i) % 3, HALF_O[i % 2],
                          bass.ds(s * 3 * GW + GW * (i // 2), GW))
        for i in range(12, 16):
            out_chunk(2 * G_O + i, (2 * G_O + i) % 3, HALF_O[i % 2],
                      slice(GW * (i // 2), GW * (i // 2 + 1)))

    def pool_program(pool):
        pool.memset(ident[:, :], 0.0).then_inc(pool_const, 1)
        pool.memset(ones[:, :], 1.0).then_inc(pool_const, 1)
        pool.iota(slots_i[:, :], [[1, P]], base=0, channel_multiplier=0).then_inc(pool_const, 1)
        pool.iota(rcount_i[:, :], [[1, 16]], base=1, channel_multiplier=0).then_inc(pool_const, 1)
        pool.memset(wsb_nat[:, :, :], 0.0).then_inc(pool_const, 1)
        pool.wait_ge(pool_const, 5)
        pool.affine_select(out=ident[:, :], in_=ident[:, :], compare_op=ALU.not_equal, fill=1.0,
                           base=0, pattern=[[-1, P]], channel_multiplier=1).then_inc(pool_const, 1)
        pool.affine_select(out=before[:, :], in_=ones[:, :], compare_op=ALU.is_gt, fill=0.0,
                           base=0, pattern=[[1, P]], channel_multiplier=-1).then_inc(pool_const, 1)
        pool.tensor_copy(slots[:, :], slots_i[:, :]).then_inc(pool_const, 1)
        pool.tensor_copy(rcount[:, :], rcount_i[:, :]).then_inc(pool_const, 1)
        pool.wait_ge(sgu_in, 16 * (1 + NB))
        pool.affine_select(out=ws_nat[:, :, :], in_=ws_nat[:, :, :], compare_op=ALU.is_ge, fill=0.0,
                           base=0, pattern=[[0, HT], [-1, P]], channel_multiplier=1)\
            .then_inc(pool_const, 1)
        pool.affine_select(out=wsb_nat[:, :, :], in_=wsb_nat[:, :, :], compare_op=ALU.is_ge,
                           fill=0.0, base=0, pattern=[[0, HT], [-1, NB * NT]],
                           channel_multiplier=1).then_inc(pool_const, 1)

    def group_products(pe, g, acts, halves, turn=0, turns_at=0, wait_half=None):
        hi, lo = acts
        pair = g % 3
        if g >= 3:
            pe.wait_ge(pair_free[pair], g // 3 + turn * (turns_at // 3))
        for n in range(2):
            if n and wait_half:
                pe.wait_ge(*wait_half)
            k = (2 * g + n) % 3
            pe.wait_ge(lo_ready, 2 * g + n + 1 + turn * (2 * turns_at))
            wh = w_hi[k][:, :].rearrange("p (t n) -> p t n", t=CK)
            wl = w_lo[k][:, :].rearrange("p (t n) -> p t n", t=CK)
            for t in range(CK):
                kt = CK * halves[n] + t
                for f in range(2):
                    out = ps[:, 2 * pair + f, 0:NTOK]
                    col = slice(P * f, P * (f + 1))
                    pe.matmul(out, wh[:, t, col], hi[:, kt, :], start=(n == 0 and t == 0), stop=False)
                    pe.matmul(out, wh[:, t, col], lo[:, kt, :], start=False, stop=False)
                    last = pe.matmul(out, wl[:, t, col], hi[:, kt, :], start=False,
                                     stop=(n == 1 and t == CK - 1))
            last.then_inc(w_used, 1)

    def pe_mixer(pe):
        def bank_of(n, add=0):
            b, full = tb(n)
            if n >= 2:
                pe.wait_ge(tb_free[b], full - 1 + add)
            return b, ps[:, TB0 + b, :]

        pe.wait_ge(pool_const, 6)
        for i, (t0, m) in enumerate(TILES):
            pe.wait_ge(x_in[i], 16)
            for q in range(4):
                b, bank = bank_of(USE[f"x{i}{q}"])
                for t in range(4):
                    last = pe.transpose(bank[:, P * t:P * t + m], tok[0:m, i, 4 * q + t::KT],
                                        ident[0:m, 0:m])
                last.then_inc(tb_full[b], 1)
        pe.wait_ge(par_in, 16 * 4)
        b, bank = bank_of(USE["par"])
        n = 3 * CT + PT
        pe.transpose(bank[:, 0:n], par_nat[:, :], ident[0:n, 0:n]).then_inc(tb_full[b], 1)
        X, Y = (xT_hi, xT_lo), (yT_hi, yT_lo)
        wait_read(pe, "x22", "x23")
        group_products(pe, 0, X, (0, 1))
        group_products(pe, 1, X, (0, 1))
        pe.wait_ge(state_in, 32)
        b, bank = bank_of(USE["spool"])
        for j in range(PT):
            last = pe.transpose(bank[:, P * j:P * j + NB * PBUF], spool_nat[:, P * j:P * (j + 1)],
                                ident[0:NB * PBUF, 0:NB * PBUF])
        last.then_inc(tb_full[b], 1)
        b, bank = bank_of(USE["sconv"])
        for j in range(CT):
            last = pe.transpose(bank[:, 2 * NB * j:2 * NB * (j + 1)], sconv_nat[:, P * j:P * (j + 1)],
                                ident[0:2 * NB, 0:2 * NB])
        last.then_inc(tb_full[b], 1)
        group_products(pe, 2, X, (0, 1))
        pe.wait_ge(diff_ready, 1)
        for j in range(PT):
            b, bank = bank_of(USE[f"pool{j}"])
            pe.matmul(bank[:, 0:NTOK], poolw[:, j, :], pdiff[:, j, :], start=True, stop=True)\
              .then_inc(tb_full[b], 1)
        b, bank = bank_of(USE["pout0"])
        for j in range(PT):
            last = pe.transpose(bank[0:16, P * j:P * (j + 1)], pext[:, j, PBUF + SEQ - 16:PBUF + SEQ],
                                ident[:, :])
        last.then_inc(tb_full[b], 1)
        b, bank = bank_of(USE["pout1"])
        for j in range(PT):
            last = pe.transpose(bank[0:64, P * j:P * (j + 1)], pnew[:, j, :], ident[:, :])
        last.then_inc(tb_full[b], 1)
        group_products(pe, 3, X, (0, 1))
        pe.wait_ge(pool_const, 11)
        for n, heads in enumerate((range(0, 4), range(4, HT))):
            b, bank = bank_of(USE[f"ws{n}"])
            for h in heads:
                last = pe.transpose(bank[:, P * (h % 4):P * (h % 4) + P], ws_nat[:, h, :], ident[:, :])
            last.then_inc(tb_full[b], 1)
        b, bank = bank_of(USE["wsb"])
        for h in range(HT):
            last = pe.transpose(bank[0:64, 64 * h:64 * (h + 1)], wsb_nat[:, h, :], ident[0:64, 0:64])
        last.then_inc(tb_full[b], 1)
        group_products(pe, 4, X, (0, 1))
        group_products(pe, 5, X, (0, 1))
        wait_group_read(pe, G_V + 2)
        for i, (t0, m) in enumerate(TILES):
            for q, heads in enumerate((range(0, 4), range(4, HT))):
                b, bank = bank_of(USE[f"v{i}{q}"])
                for h in heads:
                    last = pe.transpose(bank[0:m, P * (h % 4):P * (h % 4) + P], vT[:, h, t0:t0 + m],
                                        ident[:, :])
                last.then_inc(tb_full[b], 1)
        group_products(pe, 6, X, (0, 1))
        pe.wait_ge(vn_ready, 3)
        for h in range(HT):
            b, bank = bank_of(USE[f"mix{h}"])
            one = ones[64:65, :]
            head = slice(P * h, P * (h + 1))
            for c in range(2):
                out = bank[:, P * c:P * (c + 1)]
                pe.matmul(out, vtok[:, c, head], wsT[:, h, :], start=True, stop=False)
                pe.matmul(out, one, brow[:, h, :], start=False, stop=True)
            out = bank[:, SEQ:NTOK]
            pe.matmul(out, vtok[0:64, 2, head], wsbT[:, h, :], start=True, stop=False)
            pe.matmul(out.rearrange("p (b t) -> p b t", b=NB), one,
                      brow[:, h:h + 1, 0:NT].to_broadcast([1, NB, NT]),
                      start=False, stop=True).then_inc(tb_full[b], 1)
        group_products(pe, 7, X, (0, 1))
        with pe.Fori(0, 3) as s:
            for i in range(3):
                group_products(pe, G_H + i, X, (0, 1), s, 3)
        pe.wait_ge(z_ready, 1)
        for n, tiles in enumerate((range(0, 4), range(4, CT))):
            b, bank = bank_of(USE[f"z{n}"])
            for j in tiles:
                last = pe.transpose(bank[0:2 + 2 * NB, P * (j % 4):P * (j % 4) + P], zlast[:, j, :],
                                    ident[:, :])
            last.then_inc(tb_full[b], 1)

        def out_tokens(k, turn=0):
            wait = pair_free[(G_O + k) % 3], (G_O + k) // 3 + 1 + turn
            pe.wait_ge(*wait)
            buf = mixT[k % 3]
            n = USE_O + 2 * k
            b, bank = bank_of(n, 3 * turn)
            b2, bank2 = bank_of(n + 1, 3 * turn)
            for i in range(2):
                for f in range(2):
                    last = pe.transpose(bank[:, GW * i + P * f:GW * i + P * (f + 1)],
                                        buf[:, f, P * i:P * (i + 1)], ident[:, :])
            last.then_inc(tb_full[b], 1)
            b, bank = b2, bank2
            for f in range(2):
                last = pe.transpose(bank[0:64, P * f:P * (f + 1)], buf[:, f, SEQ:NTOK], ident[:, :])
            last.then_inc(tb_full[b], 1)

        pe.wait_ge(ylo_ready, 4)
        group_products(pe, G_O, Y, HALF_O, wait_half=(ylo_ready, 7))
        with pe.Fori(0, 2) as s:
            for i in range(3):
                group_products(pe, G_O + 1 + i, Y, HALF_O, s, 3)
                out_tokens(i, s)
        group_products(pe, G_END - 1, Y, HALF_O)
        out_tokens(6)
        out_tokens(7)

    def split_hi(act, c, turn=0, per=0):
        k = c % 3
        act.wait_ge(raw_full[k], 16 * (c // 3 + 1) + turn * (16 * per // 3))
        if c >= RING:
            act.wait_ge(w_used, c - RING + 1 + turn * per)
        act.activation(w_hi[k][:, :], raw[k][:, :], ACT.Copy).then_inc(hi_ready, 1)

    def split_lo(dve, c, turn=0, per=0):
        k = c % 3
        dve.wait_ge(hi_ready, c + 1 + turn * per)
        dve.tensor_tensor(w_lo[k][:, :], raw[k][:, :], w_hi[k][:, :].bitcast(FP32), ALU.subtract)\
           .then_inc(lo_ready, 1)

    def act_mixer(act):
        act.dma_start(par_nat[0:3 * CT, :], conv_w[0].rearrange("k (j p) -> (k j) p", p=P))\
           .then_inc(par_in, 16)
        act.dma_start(par_nat[3 * CT:3 * CT + PT, :], pool_scale[0].rearrange("(j p) -> j p", p=P))\
           .then_inc(par_in, 16)
        act.dma_start(poolw[:, :, :], pool_w[0].rearrange("g c d -> c g d")).then_inc(par_in, 16)
        act.dma_start(brow, sgu_b[0:1]).then_inc(par_in, 16)
        act.dma_start(sconv_nat[:, :], state_conv[0].rearrange("b r c -> (b r) c")).then_inc(state_in, 16)
        act.dma_start(spool_nat[:, :], state_pool[0].rearrange("b r c -> (b r) c")).then_inc(state_in, 16)
        act.dma_start(ws_nat[:, :, :], sgu_w[0].rearrange("h t s -> t h s")).then_inc(sgu_in, 16)
        act.wait_ge(pool_const, 5)
        for b in range(NB):
            act.dma_start(wsb_nat[NT * b:NT * (b + 1), :, NT * b:NT * (b + 1)],
                          sgu_w[0][:, 0:NT, 0:NT].rearrange("h t s -> t h s")).then_inc(sgu_in, 16)
        act.dma_start(sg_g[:, :], sgu_ln_g[0:1, :].to_broadcast([P, CHW])).then_inc(gb_in, 16)
        act.dma_start(sg_b[:, :], sgu_ln_b[0:1, :].to_broadcast([P, CHW])).then_inc(gb_in, 16)
        act.dma_start(new_pool_sample[0][:, 0:PBUF - NT, :], state_pool[0][:, NT:PBUF, :])\
           .then_inc(copy_out, 16)

        def copy_use(name, out, in_of):
            b, full = tb(USE[name])
            act.wait_ge(tb_full[b], full)
            act.activation(out, in_of(ps[:, TB0 + b, :]), ACT.Copy).then_inc(tb_free[b], 1)

        def copy_group(g, out):
            pair = g % 3
            act.wait_ge(w_used, 2 * g + 2)
            act.activation(out, ps[:, 2 * pair:2 * pair + 2, 0:NTOK], ACT.Copy)\
               .then_inc(pair_free[pair], 1)

        def y_hi(first, n):
            act.activation(yT_hi[:, first:first + n, :], tmp[:, 0:n, :], ACT.Copy).then_inc(yhi_ready, 1)

        for i, (t0, m) in enumerate(TILES):
            for q in range(4):
                b, full = tb(USE[f"x{i}{q}"])
                act.wait_ge(tb_full[b], full)
                act.activation(xT_hi[:, 4 * q:4 * q + 4, t0:t0 + m],
                               ps[:, TB0 + b, :].rearrange("p (t c) -> p t c", t=4)[:, :, 0:m],
                               ACT.Copy).then_inc(xhi_ready, 1)
        n = 3 * CT + PT
        copy_use("par", parT[:, :], lambda bank: bank[:, 0:n])

        def sample_new(g2, width, hist):
            return g2.rearrange("p j (b t) -> p j b t", b=NB)[:, :, :, hist:hist + NT]

        for g in range(G_O + 1):
            split_hi(act, 2 * g)
            split_hi(act, 2 * g + 1)
            if g in (1, 2):
                k = g - 1
                act.wait_ge(w_used, 2 * k + 2)
                if k == 0:
                    act.wait_ge(dve_step, 1)
                bank2 = ps[:, 2 * k:2 * k + 2, :]
                act.activation(pext[:, 2 * k:2 * k + 2, PBUF:PBUF + SEQ], bank2[:, :, 0:SEQ], ACT.Copy)\
                   .then_inc(act_step, 1)
                act.activation(pnew[:, 2 * k:2 * k + 2, :], bank2[:, :, SEQ:NTOK], ACT.Copy)\
                   .then_inc(act_step, 1)
                for f in range(2):
                    out = pext[:, 2 * k + f, PBUF + SEQ:PW].rearrange("p (b t) -> p b t", b=NB)
                    last = act.activation(out[:, :, PBUF:PBUF + NT],
                                          ps[:, 2 * k + f, SEQ:NTOK].rearrange("p (b t) -> p b t", b=NB),
                                          ACT.Copy)
                    last.then_inc(pair_free[k] if f else act_step, 1)
            if g == 2:
                for j in range(PT):
                    b, full = tb(USE["spool"])
                    act.wait_ge(tb_full[b], full)
                    out = pext[:, j, PBUF + SEQ:PW].rearrange("p (b t) -> p b t", b=NB)
                    act.activation(out[:, :, 0:PBUF],
                                   ps[:, TB0 + b, P * j:P * j + NB * PBUF].rearrange("p (b t) -> p b t", b=NB),
                                   ACT.Copy).then_inc(tb_free[b] if j == PT - 1 else act_step, 1)
                copy_use("sconv", zstate[:, :, :],
                         lambda bank: bank[:, 0:CT * 2 * NB].rearrange("p (j c) -> p j c", j=CT))
            if g == 3:
                wait_read(act, f"pool{PT - 2}", f"pool{PT - 1}")
                y_hi(12, PT)
                copy_use("pout0", p_out[:, :], lambda bank: bank[0:16, :])
                copy_use("pout1", p_out2[:, :], lambda bank: bank[0:64, :])
                wait_read(act, "pout0", "pout1")
                act.dma_start(new_pool_prompt[0, 0], p_out[1:16, :]).then_inc(small_out, 16)
                for b in range(NB):
                    act.dma_start(new_pool_sample[0, b, PBUF - NT:PBUF, :],
                                  p_out2[NT * b:NT * (b + 1), :]).then_inc(small_out, 16)
                copy_group(G_V, vT[:, 0:2, :])
            if g == 4:
                copy_use("ws0", wsT[:, 0:4, :], lambda bank: bank.rearrange("p (h c) -> p h c", h=4))
                copy_use("ws1", wsT[:, 4:HT, :],
                         lambda bank: bank[:, 0:(HT - 4) * P].rearrange("p (h c) -> p h c", h=HT - 4))
                copy_use("wsb", wsbT[:, :, :],
                         lambda bank: bank[0:64, 0:HT * 64].rearrange("p (h c) -> p h c", h=HT))
                copy_group(G_V + 1, vT[:, 2:4, :])
            if g == 5:
                copy_group(G_V + 2, vT[:, 4:6, :])
            if g == 6:
                for i, (t0, m) in enumerate(TILES):
                    copy_use(f"v{i}0", vtok[0:m, i, 0:4 * P], lambda bank: bank[0:m, :])
                    copy_use(f"v{i}1", vtok[0:m, i, 4 * P:CHW], lambda bank: bank[0:m, 0:CHW - 4 * P])
                act.wait_ge(var_ready, 1)
                act.activation(vrstd[:, :], vstd[:, :], ACT.Sqrt).then_inc(std_ready, 1)
            if g == 7:
                act.wait_ge(vn_ready, 3)
                act.dma_start(new_chunk_v[0].rearrange("b t c -> (b t) c"), vtok[0:64, 2, :])\
                   .then_inc(small_out, 16)
                for h in range(HT):
                    copy_use(f"mix{h}", mixu[:, h, :], lambda bank: bank[:, 0:NTOK])
            if g in (7, 8, 9):
                wait_group_read(act, g - 2)
                y_hi(6 + 2 * (g - 7), 2)
            if g == 10:
                act.wait_ge(small_out, 16 * (2 + NB))
            if g in (10, 11, 12):
                copy_group(g - 2, convt[:, 2 * (g - 10):2 * (g - 10) + 2, :])
            if g in (16, 17):
                wait_group_read(act, g - 2)
                y_hi(2 * (g - 16), 2)
            if g == 17:
                wait_group_read(act, g - 1)
                y_hi(4, 2)
                copy_use("z0", z_out[:, 0:4 * P], lambda bank: bank[0:2 + 2 * NB, :])
                copy_use("z1", z_out[:, 4 * P:CONV], lambda bank: bank[0:2 + 2 * NB, 0:CONV - 4 * P])
                wait_read(act, "z0", "z1")
                act.dma_start(new_conv_prompt[0, 0], z_out[0:2, :]).then_inc(small_out, 16)
                act.dma_start(new_conv_sample[0].rearrange("b r c -> (b r) c"), z_out[2:2 + 2 * NB, :])\
                   .then_inc(small_out, 16)
                act.dma_start(lng[:, :], ln1_g[0:1, :].to_broadcast([P, D])).then_inc(gb_in, 16)
                act.dma_start(lnb[:, :], ln1_b[0:1, :].to_broadcast([P, D])).then_inc(gb_in, 16)
                act.dma_start(rg_nat[:, :, :], rg_w[0].rearrange("(p t) n -> p t n", t=KT)).then_inc(rw_in, 16)
                act.dma_start(re_nat[:, :, :], re_w[0].rearrange("(p t) n -> p t n", t=KT)).then_inc(rw_in, 16)
                act.dma_start(rbias[:, 0:NG], rg_b[0:1, :]).then_inc(rw_in, 16)
                act.dma_start(rbias[:, NG:NG + NE], re_b[0:1, :]).then_inc(rw_in, 16)

        def copy_out_group(k, turn=0):
            g = G_O + k
            pair = g % 3
            act.wait_ge(w_used, 2 * g + 2 + 6 * turn)
            if k >= 3 or not isinstance(turn, int):
                b, full = tb(USE_O + 2 * k + 1)
                act.wait_ge(tb_full[b], full - 3 + 3 * turn)
            act.activation(mixT[k % 3][:, :, :], ps[:, 2 * pair:2 * pair + 2, 0:NTOK], ACT.Copy)\
               .then_inc(pair_free[pair], 1)

        with act.Fori(0, 2) as s:
            for i in range(3):
                split_hi(act, 2 * (G_O + 1 + i), s, 6)
                split_hi(act, 2 * (G_O + 1 + i) + 1, s, 6)
                copy_out_group(i, s)
        split_hi(act, 2 * G_END - 2)
        split_hi(act, 2 * G_END - 1)
        copy_out_group(6)
        copy_out_group(7)
        act.wait_ge(var_ready, 2)
        act.activation(vrstd[:, :], vstd[:, :], ACT.Sqrt).then_inc(std_ready, 1)

    def dve_mixer(dve):
        steps = Tally(dve_step)

        def link(instruction):
            dve.wait_ge(dve_step, steps.inc(instruction))

        def y_lo(first, n, count):
            dve.wait_ge(yhi_ready, count)
            dve.tensor_tensor(yT_lo[:, first:first + n, :], tmp[:, 0:n, :],
                              yT_hi[:, first:first + n, :].bitcast(FP32), ALU.subtract)\
               .then_inc(ylo_ready, 1)
            dve.wait_ge(ylo_ready, count)

        def norm_scale(n_tiles=3):
            steps_before = var_ready
            dve.tensor_scalar(vstd[:, :], vmv[:, :, 1], EPS, None, ALU.add).then_inc(var_ready, 1)

        link(dve.memset(pext[:, :, :], 0.0))
        link(dve.memset(vmv[:, :, :], 1.0))
        dve.wait_ge(pool_const, 9)
        link(dve.reciprocal(rcount[:, :], rcount[:, :]))
        for i, (t0, m) in enumerate(TILES):
            for q in range(4):
                b, full = tb(USE[f"x{i}{q}"])
                dve.wait_ge(xhi_ready, 4 * i + q + 1)
                dve.tensor_tensor(xT_lo[:, 4 * q:4 * q + 4, t0:t0 + m],
                                  ps[:, TB0 + b, :].rearrange("p (t c) -> p t c", t=4)[:, :, 0:m],
                                  xT_hi[:, 4 * q:4 * q + 4, t0:t0 + m].bitcast(FP32), ALU.subtract)\
                   .then_inc(tb_free[b], 1)

        def samples(t, j, hist):
            return t[:, j, hist + SEQ:].rearrange("p (b t) -> p b t", b=NB)

        def new(t):
            return t[:, SEQ:NTOK].rearrange("p (b t) -> p b t", b=NB)

        for g in range(G_O + 2):
            split_lo(dve, 2 * g)
            split_lo(dve, 2 * g + 1)
            if g == 2:
                wait_read(dve, "spool")
                wait_group_read(dve, 1)
                wait_group_read(dve, 0)
                src, w = pext, 1
                for n, dst in enumerate((sum_a, sum_b, sum_a, sum_b)):
                    lo_ = 2 * w - 1
                    link(dve.tensor_tensor(dst[:, n:PT, lo_:PW], src[:, n:PT, lo_:PW],
                                           src[:, n:PT, lo_ - w:PW - w], ALU.add))
                    w *= 2
                    s_ = dst
                    link(dve.scalar_tensor_tensor(
                        out=pdiff[:, n, w - 1:SEQ], in0=s_[:, n, PBUF + w - 1:PBUF + SEQ],
                        scalar=1.0 / w, in1=pext[:, n, PBUF + w - 1:PBUF + SEQ],
                        op0=ALU.mult, op1=ALU.subtract))
                    link(dve.tensor_tensor(pdiff[:, n, 0:w - 1], s_[:, n, PBUF:PBUF + w - 1],
                                           rcount[:, 0:w - 1], ALU.mult))
                    link(dve.tensor_tensor(pdiff[:, n, 0:w - 1], pdiff[:, n, 0:w - 1],
                                           pext[:, n, PBUF:PBUF + w - 1], ALU.subtract))
                    last = dve.scalar_tensor_tensor(
                        out=new(pdiff[:, n, :]), in0=samples(s_, n, PBUF)[:, :, PBUF:PBUF + NT],
                        scalar=1.0 / w, in1=samples(pext, n, PBUF)[:, :, PBUF:PBUF + NT],
                        op0=ALU.mult, op1=ALU.subtract)
                    if n < PT - 1:
                        link(last)
                    else:
                        last.then_inc(diff_ready, 1)
                    src = dst
            if g == 3:
                wait_read(dve, "par")
                for j in range(PT):
                    b, full = tb(USE[f"pool{j}"])
                    dve.wait_ge(tb_full[b], full)
                    dve.tensor_scalar(tmp[:, j, :], ps[:, TB0 + b, 0:NTOK],
                                      parT[:, 3 * CT + j:3 * CT + j + 1], None, ALU.mult)\
                       .then_inc(tb_free[b], 1)
                y_lo(12, PT, 1)
            if g == 6:
                dve.wait_ge(gb_in, 32)
                for i, (t0, m) in enumerate(TILES):
                    wait_read(dve, f"v{i}0", f"v{i}1")
                    for q in range(2):
                        link(dve.bn_stats(vstats[0:m, i, q, :], vtok[0:m, i, CHW // 2 * q:CHW // 2 * (q + 1)]))
                    link(dve.bn_aggr(vmv[0:m, i, :], vstats[0:m, i, :, :].rearrange("p a b -> p (a b)")))
                norm_scale()
                dve.wait_ge(std_ready, 1)
                link(dve.reciprocal(vrstd[:, :], vrstd[:, :]))
                for i, (t0, m) in enumerate(TILES):
                    link(dve.scalar_tensor_tensor(out=vtok[0:m, i, :], in0=vtok[0:m, i, :],
                                                  scalar=vmv[0:m, i, 0:1], in1=sg_g[0:m, :],
                                                  op0=ALU.subtract, op1=ALU.mult))
                    dve.scalar_tensor_tensor(out=vtok[0:m, i, :], in0=vtok[0:m, i, :],
                                             scalar=vrstd[0:m, i:i + 1], in1=sg_b[0:m, :],
                                             op0=ALU.mult, op1=ALU.add).then_inc(vn_ready, 1)
            if g in (7, 8, 9):
                k, pair = g - 7, (g - 2) % 3
                wait_read(dve, f"mix{2 * k}", f"mix{2 * k + 1}")
                dve.wait_ge(w_used, 2 * (g - 2) + 2)
                dve.tensor_tensor(tmp[:, 0:2, :], ps[:, 2 * pair:2 * pair + 2, 0:NTOK],
                                  mixu[:, 2 * k:2 * k + 2, :], ALU.mult).then_inc(pair_free[pair], 1)
                y_lo(6 + 2 * k, 2, 2 + k)
            if g == 12:
                dve.wait_ge(small_out, 16 * (2 + NB))
                dve.wait_ge(vn_ready, 3)
                link(dve.memset(zext[:, :, 0:2], 0.0))
                for r in range(2):
                    link(dve.tensor_copy(
                        zext[:, :, 2 + SEQ:ZW].rearrange("p j (b t) -> p j b t", b=NB)[:, :, :, r],
                        zstate[:, :, :].rearrange("p j (b r) -> p j b r", b=NB)[:, :, :, r]))
            if g in (13, 14, 15):
                k, pair = g - 13, (g - 2) % 3
                wait_group_read(dve, G_H + k)
                dve.wait_ge(w_used, 2 * (g - 2) + 2)
                two = slice(2 * k, 2 * k + 2)
                link(dve.tensor_tensor(zext[:, two, 2:2 + SEQ], ps[:, 2 * pair:2 * pair + 2, 0:SEQ],
                                       convt[:, two, 0:SEQ], ALU.mult))
                for f in range(2):
                    last = dve.tensor_tensor(samples(zext, 2 * k + f, 2)[:, :, 2:2 + NT],
                                             new(ps[:, 2 * pair + f, :]), new(convt[:, 2 * k + f, :]),
                                             ALU.mult)
                    if f == 0:
                        link(last)
                last.then_inc(pair_free[pair], 1)
                wait_group_read(dve, g - 2)
                for j in (2 * k, 2 * k + 1):
                    for out, ext in ((convt[:, j, 0:SEQ], lambda r: zext[:, j, r:r + SEQ]),
                                     (new(convt[:, j, :]), lambda r: samples(zext, j, 2)[:, :, r:r + NT])):
                        link(dve.tensor_scalar(out, ext(0), parT[:, j:j + 1], None, ALU.mult))
                        for r in (1, 2):
                            link(dve.scalar_tensor_tensor(out=out, in0=ext(r),
                                                          scalar=parT[:, CT * r + j:CT * r + j + 1],
                                                          in1=out, op0=ALU.mult, op1=ALU.add))
            if g == 15:
                link(dve.tensor_copy(zlast[:, :, 0:2], zext[:, :, SEQ:SEQ + 2]))
                for r in range(2):
                    last = dve.tensor_copy(
                        zlast[:, :, 2:].rearrange("p j (b r) -> p j b r", b=NB)[:, :, :, r],
                        zext[:, :, 2 + SEQ:ZW].rearrange("p j (b t) -> p j b t", b=NB)[:, :, :, NT + r])
                    if r == 0:
                        link(last)
                last.then_inc(z_ready, 1)
            for k in {16: (0,), 17: (1, 2)}.get(g, ()):
                src = G_B + k
                pair = src % 3
                dve.wait_ge(w_used, 2 * src + 2)
                dve.tensor_tensor(tmp[:, 0:2, :], ps[:, 2 * pair:2 * pair + 2, 0:NTOK],
                                  convt[:, 2 * k:2 * k + 2, :], ALU.mult).then_inc(pair_free[pair], 1)
                y_lo(2 * k, 2, 5 + k)

        def residual(k, turn=0):
            n = USE_O + 2 * k
            col = slice(GW * k, GW * (k + 1)) if isinstance(turn, int) else \
                bass.ds(turn * (3 * GW) + GW * k, GW)
            b, full = tb(n)
            dve.wait_ge(tb_full[b], full + 3 * turn)
            dve.scalar_tensor_tensor(out=tok[:, 0:2, col], in0=tok[:, 0:2, col], scalar=ALPHA,
                                     in1=ps[:, TB0 + b, :].rearrange("p (i c) -> p i c", i=2),
                                     op0=ALU.mult, op1=ALU.add).then_inc(tb_free[b], 1)
            b2, full2 = tb(n + 1)
            dve.wait_ge(tb_full[b2], full2 + 3 * turn)
            dve.scalar_tensor_tensor(out=tok[0:64, 2, col], in0=tok[0:64, 2, col], scalar=ALPHA,
                                     in1=ps[0:64, TB0 + b2, 0:GW], op0=ALU.mult, op1=ALU.add)\
               .then_inc(tb_free[b2], 1)
            dve.wait_ge(tb_free[b], full + 3 * turn)
            dve.wait_ge(tb_free[b2], full2 + 3 * turn)
            kk = k if isinstance(turn, int) else 3 * turn + k
            for i, (t0, m) in enumerate(TILES):
                out = xstats[0:m, i, bass.ds(kk, 1), :].rearrange("p a b -> p (a b)") \
                    if not isinstance(turn, int) else xstats[0:m, i, kk, :]
                steps.inc(dve.bn_stats(out, tok[0:m, i, col]))

        with dve.Fori(0, 2) as s:
            steps.enter(s, 9)
            for i in range(3):
                split_lo(dve, 2 * (G_O + 2 + i), s, 6)
                split_lo(dve, 2 * (G_O + 2 + i) + 1, s, 6)
                residual(i, s)
        steps.leave(2)
        residual(6)
        residual(7)
        dve.wait_ge(dve_step, steps.value)
        for i, (t0, m) in enumerate(TILES):
            link(dve.bn_aggr(vmv[0:m, i, :], xstats[0:m, i, :, :].rearrange("p a b -> p (a b)")))
        norm_scale()
        dve.wait_ge(std_ready, 2)
        link(dve.reciprocal(vrstd[:, :], vrstd[:, :]))
        return steps, link

    RAW_BASE = [0, 0, 0]
    for c in range(CHUNKS1):
        RAW_BASE[c % 3] += 1

    def raw_slot(j):
        k = (j + 3) % 6
        return k, RAW_BASE[k] if k < 3 else 0

    def x_use(n, q):
        b, full = tb(USE_E + q)
        return b, full + 2 * n

    def each_expert(eng, r, step):
        with eng.Fori(0, NE - 1) as e:
            step(r * NE + e, e, False)
        step(r * NE + NE - 1, NE - 1, True)

    def each_round(eng, one_round):
        one_round(0)
        eng.wait_ge(facts_ready, 1)
        most = eng.value_load(fullest[0:1, 0:1], min_val=0, max_val=NTOK)
        with eng.Fori(1, ROUNDS) as r:
            with eng.If(most > r * C):
                one_round(r)

    gate_v = w_gate[0].rearrange("e (p t) f -> p e t f", t=KT)
    up_v = w_up[0].rearrange("e (p t) f -> p e t f", t=KT)
    down_v = w_down[0].rearrange("e (j p) d -> p e j d", p=P)
    FH = F // 2

    def sp_expert(sp, n, e, first):
        one = bass.ds(e, 1)
        for j in range(ECH):
            k, base_ = raw_slot(j)
            if first and j == 3:
                sp.wait_ge(lo_ready, CHUNKS1)
            wait_alone(sp, lo_ready, CHUNKS1 - 5 + j + n * ECH, sp_turns)
            if j < 4:
                dst, src = raw[k][:, :].rearrange("p (t f) -> p t f", t=4), gate_v[:, one, 4 * j:4 * j + 4, :]
            elif j < 8:
                h, t = (j - 4) // 2, 8 * (j % 2)
                dst = raw[k][:, :].rearrange("p (t f) -> p t f", t=8)
                src = up_v[:, one, t:t + 8, FH * h:FH * (h + 1)]
            else:
                dst, src = raw[k][:, :].rearrange("p (j d) -> p j d", j=1), down_v[:, one, j - 8:j - 7, :]
            sp.dma_start(dst, src.rearrange("p e t f -> p (e t) f")).then_inc(raw_full[k], 16)

    def sp_experts(sp):
        sp.wait_ge(ylo_ready, 7)
        sp.wait_ge(small_out, 16 * (4 + NB))
        sp_expert(sp, 0, 0, True)
        with sp.Fori(1, NE) as e:
            sp_expert(sp, e, e, False)
        sp.wait_ge(facts_ready, 1)
        most = sp.value_load(fullest[0:1, 0:1], min_val=0, max_val=NTOK)
        with sp.Fori(1, ROUNDS) as r:
            with sp.If(most > r * C):
                with sp.Fori(0, NE) as e:
                    sp_expert(sp, r * NE + e, e, False)

    def sp_finish(sp):
        sp.wait_ge(experts_done, 1)
        for i, (t0, m) in enumerate(TILES):
            sp.dma_start(yrows[i][0:m, :, :], y_dram.rearrange("(t w) d -> t w d", w=2)[t0:t0 + m])\
              .then_inc(fin_in[i], 16)
        y_tiles = [y_prompt[0, 0:P, :], y_prompt[0, P:SEQ, :], y_sample.rearrange("b t d -> (b t) d")]
        for i, (t0, m) in enumerate(TILES):
            sp.wait_ge(fin_ready, i + 1)
            sp.dma_start(y_tiles[i], tok[0:m, i, :]).then_inc(y_out, 16)
        sp.wait_ge(y_out, 16 * 3)
        sp.wait_ge(copy_out, 16)
        sp.wait_ge(small_out, 16 * (4 + NB))

    def pool_experts(pool):
        pool.wait_ge(ylo_ready, 7)
        pool.iota(token_i[:, :], [[P, 3]], base=-int(BIG), channel_multiplier=1).then_inc(pool_const, 1)
        pool.iota(first_i[:, :], [[-1, EG]], base=EG, channel_multiplier=0).then_inc(pool_const, 1)
        pool.wait_ge(pool_const, 13)
        pool.tensor_copy(token[:, :], token_i[:, :]).then_inc(pool_const, 1)
        pool.tensor_copy(first_w[:, :], first_i[:, :]).then_inc(pool_const, 1)
        pool.wait_ge(w_used, CHUNKS1)
        pool.memset(xg[:, :], 0.0).then_inc(xg_zero, 1)
        pool.wait_ge(xg_zero, 1)
        pool.sem_inc(yout_free, 1)
        pool.wait_ge(x1_stored, 16 * 3)

        def gather(n):
            wait_alone(pool, rows_ready, n + 1, pool_turns)
            pool.indirect_dma_start(
                out=xg[:, :], out_offset=None, in_=x1_dram,
                in_offset=bass.IndirectOffsetOnAxis(ap=gather_row[:, 0:1], axis=0),
                bounds_check=NTOK - 1, oob_is_err=False).then_inc(gathered, 16)

        def step(n, e, last):
            if not last:
                gather(n + 1)
            pool.tensor_copy(result_row[:, :], result_rows[:, bass.ds(n, 1)])\
                .then_inc(result_row_ready, 1)
            wait_alone(pool, result_row_ready, n + 1, pool_turns)
            wait_alone(pool, y_read, n + 2, pool_turns)
            pool.indirect_dma_start(
                out=y_dram, out_offset=bass.IndirectOffsetOnAxis(ap=result_row[:, 0:1], axis=0),
                in_=yout[:, :], in_offset=None,
                bounds_check=2 * NTOK - 1, oob_is_err=False).then_inc(scattered, 16)
            pool.wait_ge(scattered, 16 * n + 16)
            pool.sem_inc(yout_free, 1)

        def one_round(r):
            gather(r * NE)
            each_expert(pool, r, step)

        each_round(pool, one_round)
        pool.sem_inc(experts_done, 1)

    def pe_router(pe):
        pe.wait_ge(rw_ready, 1)
        for i, (t0, m) in enumerate(TILES):
            pe.wait_ge(x1_ready, i + 1)
            for q in range(4):
                b, full = tb(USE[f"r{i}{q}"])
                pe.wait_ge(tb_free[b], full - 1)
                for t in range(4):
                    last = pe.transpose(ps[:, TB0 + b, P * t:P * t + m], tok[0:m, i, 4 * q + t::KT],
                                        ident[0:m, 0:m])
                last.then_inc(tb_full[b], 1)
            wait_read(pe, f"r{i}2", f"r{i}3")
            b, full = tb(USE[f"lg{i}"])
            out = ps[0:m, TB0 + b, 0:NG + NE]
            for kt in range(KT):
                pe.matmul(out, x1T[:, kt, t0:t0 + m], rw[:, kt, :], start=(kt == 0), stop=False)
            pe.matmul(out, ones[0:1, 0:m], rbias[:, :], start=False, stop=True).then_inc(tb_full[b], 1)
        pe.wait_ge(mask_ready, 1)
        b, full = tb(USE["pos"])
        pe.wait_ge(tb_free[b], full - 1)
        mask = r16[2]
        for i, (t0, m) in enumerate(TILES):
            out = ps[0:m, TB0 + b, NE * i:NE * (i + 1)]
            for i2 in range(i):
                pe.matmul(out, ones[:, 0:m], mask[:, i2, :], start=(i2 == 0), stop=False)
            pe.matmul(out, before[0:m, 0:m], mask[0:m, i, :], start=(i == 0), stop=True)
        out = ps[:, TB0 + b, 3 * NE:4 * NE]
        for i, (t0, m) in enumerate(TILES):
            last = pe.matmul(out, ones[0:m, :], mask[0:m, i, :], start=(i == 0), stop=(i == 2))
        last.then_inc(tb_full[b], 1)

    GATE, UP, DOWN = 0, 1, 2
    HALF = (UP, GATE)

    def pe_experts(pe):
        def slots(n, e):
            pe.wait_ge(onehot_ready, n + 1)
            for i, (t0, m) in enumerate(TILES):
                fact = facts[0:m, i, e, :] if isinstance(e, int) else \
                    facts[0:m, i, bass.ds(e, 1), :].rearrange("p a b -> p (a b)")
                last = pe.matmul(ps[:, UP, 0:3], onehot[0:m, i, :], fact, start=(i == 0), stop=(i == 2))
            last.then_inc(slots_made, 1)

        def tokens(n, q):
            b, full = x_use(n, q)
            if q == 0:
                pe.wait_ge(gathered, 16 * n + 16)
            pe.wait_ge(tb_free[b], full - 1)
            for t in range(4):
                last = pe.transpose(ps[:, TB0 + b, P * t:P * (t + 1)], xg[:, 4 * q + t::KT], ident[:, :])
            last.then_inc(tb_full[b], 1)

        def split_product(out, x, w, start, stop):
            pe.matmul(out, x[0], w[0], start=start, stop=False)
            pe.matmul(out, x[1], w[0], start=False, stop=False)
            return pe.matmul(out, x[0], w[1], start=False, stop=stop)

        def step(n, e, last_step):
            for j in range(ECH):
                k = (CHUNKS1 + j) % 3
                pe.wait_ge(lo_ready, CHUNKS1 + j + 1 + n * ECH)
                if j < 4:
                    b, full = x_use(n, j)
                    pe.wait_ge(tb_free[b], full)
                    wh = w_hi[k][:, :].rearrange("p (t f) -> p t f", t=4)
                    wl = w_lo[k][:, :].rearrange("p (t f) -> p t f", t=4)
                    for t in range(4):
                        kt = 4 * j + t
                        last = split_product(ps[:, GATE, :], (xgT_hi[:, kt, :], xgT_lo[:, kt, :]),
                                             (wh[:, t, :], wl[:, t, :]), kt == 0, kt == KT - 1)
                elif j < 8:
                    if j == 4 and not last_step:
                        pe.wait_ge(rows_ready, n + 2)
                    if j == 6:
                        pe.wait_ge(silu_ready, n + 1)
                    h = (j - 4) // 2
                    wh = w_hi[k][:, :].rearrange("p (t f) -> p t f", t=8)
                    wl = w_lo[k][:, :].rearrange("p (t f) -> p t f", t=8)
                    for t in range(8):
                        kt = 8 * (j % 2) + t
                        last = split_product(ps[:, HALF[h], 0:FH],
                                             (xgT_hi[:, kt, :], xgT_lo[:, kt, :]),
                                             (wh[:, t, :], wl[:, t, :]), kt == 0, kt == KT - 1)
                else:
                    f = j - 8
                    if f == 0:
                        pe.wait_ge(y_read, n + 1)
                    if f % 2 == 0:
                        pe.wait_ge(aT_lo_ready, 2 * n + f // 2 + 1)
                    for q in range(4):
                        col = slice(512 * q, 512 * (q + 1))
                        last = split_product(ps[:, DOWN + q, :], (aT_hi[:, f, :], aT_lo[:, f, :]),
                                             (w_hi[k][:, col], w_lo[k][:, col]), f == 0, f == FT - 1)
                last.then_inc(w_used, 1)
                if j == 0 and not last_step:
                    slots(n + 1, e + 1)
                if j in (6, 8):
                    h = (j - 6) // 2
                    pe.wait_ge(a_ready, 2 * n + h + 1)
                    for t in range(2):
                        f = 2 * h + t
                        last = pe.transpose(ps[:, HALF[h], P * t:P * (t + 1)], a_sb[:, P * f:P * (f + 1)],
                                            ident[:, :])
                    last.then_inc(aT_full, 1)
                if j >= 8 and not last_step:
                    tokens(n + 1, j - 8)

        def one_round(r):
            n = r * NE
            slots(n, 0)
            for q in range(4):
                tokens(n, q)
            each_expert(pe, r, step)

        each_round(pe, one_round)

    def act_router(act):
        act.wait_ge(rw_in, 16 * 4)
        act.activation(rw[:, :, 0:NG], rg_nat[:, :, :], ACT.Copy)
        act.activation(rw[:, :, NG:NG + NE], re_nat[:, :, :], ACT.Copy).then_inc(rw_ready, 1)
        for j in range(LEAD):
            expert_hi(act, 0, j)
        for i, (t0, m) in enumerate(TILES):
            for q in range(4):
                b, full = tb(USE[f"r{i}{q}"])
                act.wait_ge(tb_full[b], full)
                act.activation(x1T[:, 4 * q:4 * q + 4, t0:t0 + m],
                               ps[:, TB0 + b, :].rearrange("p (t c) -> p t c", t=4)[:, :, 0:m],
                               ACT.Copy).then_inc(tb_free[b], 1)
            act.wait_ge(x1_ready, i + 1)
            act.dma_start(x1_dram[t0:t0 + m, :], tok[0:m, i, :]).then_inc(x1_stored, 16)
        act.dma_start(lng[:, :], ln2_g[0:1, :].to_broadcast([P, D])).then_inc(ln2_in, 16)
        act.dma_start(lnb[:, :], ln2_b[0:1, :].to_broadcast([P, D])).then_inc(ln2_in, 16)
        for n, t in enumerate((r4[0], r4[3])):
            act.wait_ge(gexp_in, n + 1)
            act.activation(t[:, :, :], t[:, :, :], ACT.Exp).then_inc(gexp_out, 1)

    def expert_hi(act, n, j):
        k = (CHUNKS1 + j) % 3
        jj, ahead = j % ECH, j // ECH
        s, base_ = raw_slot(jj)
        act.wait_ge(raw_full[s], 16 * (base_ + jj // 6 + 1 + 2 * ahead) + n * 32)
        act.wait_ge(w_used, CHUNKS1 + j - 2 + n * ECH)
        act.activation(w_hi[k][:, :], raw[s][:, :], ACT.Copy).then_inc(hi_ready, 1)

    def act_experts(act):
        act.sem_inc(y_read, 1)

        def tokens_hi(n, q):
            b, full = x_use(n, q)
            act.wait_ge(tb_full[b], full)
            act.activation(xgT_hi[:, 4 * q:4 * q + 4, :],
                           ps[:, TB0 + b, :].rearrange("p (t c) -> p t c", t=4), ACT.Copy)\
               .then_inc(xg_hi_ready, 1)

        def step(n, e, last_step):
            for j in range(LEAD, ECH + (0 if last_step else LEAD)):
                expert_hi(act, n, j)
                if j == 6:
                    act.activation(silu[:, :], ps[:, GATE, :], ACT.Silu).then_inc(silu_ready, 1)
                if j in (9, 11):
                    h = (j - 9) // 2
                    act.wait_ge(aT_full, 2 * n + h + 1)
                    act.activation(aT_hi[:, 2 * h:2 * h + 2, :],
                                   ps[:, HALF[h], 0:FH].rearrange("p (t c) -> p t c", t=2),
                                   ACT.Copy).then_inc(aT_hi_ready, 1)
                if j >= 11 and not last_step:
                    tokens_hi(n + 1, j - 11)
            act.wait_ge(w_used, CHUNKS1 + ECH + n * ECH)
            act.wait_ge(yout_free, n + 1)
            for q in range(2):
                last = act.activation(yout[:, 1024 * q:1024 * (q + 1)].rearrange("p (b c) -> p b c", b=2),
                                      ps[:, DOWN + 2 * q:DOWN + 2 * q + 2, :], ACT.Copy)
            last.then_inc(y_read, 1)

        def one_round(r):
            if not isinstance(r, int):
                for j in range(LEAD):
                    expert_hi(act, r * NE, j)
            for q in range(4):
                tokens_hi(r * NE, q)
            each_expert(act, r, step)

        each_round(act, one_round)

    def act_finish(act):
        for i in range(3):
            act.wait_ge(fin_sum, i + 1)
            act.activation(vrstd[:, i:i + 1], vstd[:, i:i + 1], ACT.Sqrt).then_inc(fin_std, 1)

    def dve_router(dve, steps, link):
        link(dve.memset(logits[:, :, :], 0.0))
        dve.wait_ge(gb_in, 64)
        for i, (t0, m) in enumerate(TILES):
            link(dve.scalar_tensor_tensor(out=tok[0:m, i, :], in0=tok[0:m, i, :],
                                          scalar=vmv[0:m, i, 0:1], in1=lng[0:m, :],
                                          op0=ALU.subtract, op1=ALU.mult))
            dve.scalar_tensor_tensor(out=tok[0:m, i, :], in0=tok[0:m, i, :],
                                     scalar=vrstd[0:m, i:i + 1], in1=lnb[0:m, :],
                                     op0=ALU.mult, op1=ALU.add).then_inc(x1_ready, 1)
        for j in range(LEAD):
            expert_lo(dve, 0, j)
        for i, (t0, m) in enumerate(TILES):
            b, full = tb(USE[f"lg{i}"])
            dve.wait_ge(tb_full[b], full)
            dve.tensor_copy(logits[0:m, i, :], ps[0:m, TB0 + b, 0:NG + NE]).then_inc(tb_free[b], 1)
            dve.wait_ge(tb_free[b], full)

        def tt(out, a, b, op):
            link(dve.tensor_tensor(out, a, b, op))

        def wide(t, n=4):
            return t[:, :, :].to_broadcast([P, 3, n])

        def top(values, most, out, s):
            link(dve.tensor_reduce(most[:, :, :], values, AXX, ALU.max))
            tt(out[:, :, :], values, wide(most), ALU.is_equal)
            tt(out[:, :, :], out[:, :, :], first_w[:, :].unsqueeze(1).to_broadcast([P, 3, EG]), ALU.mult)
            link(dve.tensor_reduce(s[:, :, :], out[:, :, :], AXX, ALU.max))
            tt(out[:, :, :], out[:, :, :], wide(s), ALU.is_equal)

        dve.wait_ge(pool_const, 15)
        glog, elog = logits[:, :, 0:NG], logits[:, :, NG:NG + NE]
        gexp, goh, e_sel, eexp, oh1, oh2 = r4
        gmax, s1, gval, emax, p1, p2, ra, rb = r1
        top(glog, gmax, goh, s1)
        link(dve.tensor_tensor(gexp[:, :, :], glog, wide(gmax), ALU.subtract))
        dve.sem_inc(gexp_in, 1)
        prod, msk1, mask, gate16 = r16

        def by(t, pattern):
            return t[:, :, :].rearrange(f"p i (g j) -> {pattern}", g=NG)

        def pick(t, axis):
            return t[:, :, :].unsqueeze(axis).to_broadcast([P, 3, NG, EG])

        tt(by(prod, "p i g j"), elog.rearrange("p i (g j) -> p i g j", g=NG), pick(goh, 3), ALU.mult)
        link(dve.tensor_reduce(e_sel[:, :, :], by(prod, "p i j g"), AXX, ALU.add))
        link(dve.tensor_reduce(emax[:, :, :], e_sel[:, :, :], AXX, ALU.max))
        tt(eexp[:, :, :], e_sel[:, :, :], wide(emax), ALU.subtract)
        dve.sem_inc(gexp_in, 1)
        dve.wait_ge(gexp_out, 2)
        link(dve.tensor_reduce(gval[:, :, :], gexp[:, :, :], AXX, ALU.add))
        link(dve.reciprocal(gval[:, :, :], gval[:, :, :]))
        link(dve.tensor_reduce(ra[:, :, :], eexp[:, :, :], AXX, ALU.add))
        link(dve.reciprocal(ra[:, :, :], ra[:, :, :]))
        tt(eexp[:, :, :], eexp[:, :, :], wide(ra), ALU.mult)
        top(eexp[:, :, :], p1, oh1, s1)
        link(dve.scalar_tensor_tensor(out=e_sel[:, :, :].rearrange("p i j -> p (i j)"),
                                      in0=oh1[:, :, :].rearrange("p i j -> p (i j)"), scalar=-2.0,
                                      in1=eexp[:, :, :].rearrange("p i j -> p (i j)"),
                                      op0=ALU.mult, op1=ALU.add))
        top(e_sel[:, :, :], p2, oh2, s1)
        tt(by(msk1, "p i g j"), pick(goh, 3), pick(oh1, 2), ALU.mult)
        tt(by(prod, "p i g j"), pick(goh, 3), pick(oh2, 2), ALU.mult)
        dve.tensor_tensor(mask[:, :, :], msk1[:, :, :], prod[:, :, :], ALU.add).then_inc(mask_ready, 1)
        tt(ra[:, :, :], p1[:, :, :], p2[:, :, :], ALU.add)
        link(dve.reciprocal(ra[:, :, :], ra[:, :, :]))
        tt(p1[:, :, :], p1[:, :, :], ra[:, :, :], ALU.mult)
        tt(p2[:, :, :], p2[:, :, :], ra[:, :, :], ALU.mult)
        tt(p1[:, :, :], p1[:, :, :], gval[:, :, :], ALU.mult)
        tt(p2[:, :, :], p2[:, :, :], gval[:, :, :], ALU.mult)
        tt(msk1[:, :, :], msk1[:, :, :], wide(p1, NE), ALU.mult)
        tt(gate16[:, :, :], prod[:, :, :], wide(p2, NE), ALU.mult)
        tt(facts[:, :, 0:NE, 2], gate16[:, :, :], msk1[:, :, :], ALU.add)
        dve.wait_ge(pool_const, 15)
        link(dve.tensor_copy(facts[:, :, :, 0], token[:, :].unsqueeze(2).to_broadcast([P, 3, NE])))
        link(dve.scalar_tensor_tensor(out=facts[:, :, :, 1],
                                      in0=token[:, :].unsqueeze(2).to_broadcast([P, 3, NE]),
                                      scalar=2.0, in1=prod[:, :, :], op0=ALU.mult, op1=ALU.add))
        link(dve.tensor_scalar(facts[:, :, :, 1], facts[:, :, :, 1], BIG, None, ALU.add))
        b, full = tb(USE["pos"])
        dve.wait_ge(tb_full[b], full)
        dve.wait_ge(mask_ready, 1)
        for i, n in ((slice(0, 2), P), (slice(2, 3), 64)):
            link(dve.scalar_tensor_tensor(
                out=gate16[0:n, i, :],
                in0=ps[0:n, TB0 + b, 0:3 * NE].rearrange("p (i e) -> p i e", i=3)[:, i, :],
                scalar=1.0, in1=mask[0:n, i, :], op0=ALU.add, op1=ALU.mult))
        for r in range(ROUNDS):
            link(dve.tensor_scalar(rank[:, :, NE * r:NE * (r + 1)], gate16[:, :, :],
                                   -1.0 - C * r, None, ALU.add))
        link(dve.tensor_reduce(r1[0][:, 0, :], ps[:, TB0 + b, 3 * NE:4 * NE], AXX, ALU.max))
        link(dve.tensor_copy(fullest[:, 0:1], r1[0][:, 0, :]))
        dve.sem_inc(tb_free[b], 1)
        dve.sem_inc(facts_ready, 1)

    def expert_lo(dve, n, j):
        k = (CHUNKS1 + j) % 3
        s, _ = raw_slot(j % ECH)
        dve.wait_ge(hi_ready, CHUNKS1 + j + 1 + n * ECH)
        dve.tensor_tensor(w_lo[k][:, :], raw[s][:, :], w_hi[k][:, :].bitcast(FP32), ALU.subtract)\
           .then_inc(lo_ready, 1)

    def dve_experts(dve):
        def place(n):
            dve.tensor_tensor(onehot[:, :, :], slots[:, :].unsqueeze(1).to_broadcast([P, 3, C]),
                              rank[:, :, bass.ds(n, 1)].to_broadcast([P, 3, C]), ALU.is_equal)\
               .then_inc(onehot_ready, 1)

        def rows(n):
            dve.wait_ge(slots_made, n + 1)
            dve.tensor_scalar(gather_row[:, :], ps[:, UP, 0:1], BIG, None, ALU.add)
            dve.tensor_scalar(result_rows[:, bass.ds(n, 1)], ps[:, UP, 1:2], BIG, None, ALU.add)
            dve.tensor_copy(gates[:, bass.ds(n, 1)], ps[:, UP, 2:3]).then_inc(rows_ready, 1)

        def tokens_lo(n, q):
            b, full = x_use(n, q)
            dve.wait_ge(xg_hi_ready, 4 * n + q + 1)
            dve.tensor_tensor(xgT_lo[:, 4 * q:4 * q + 4, :],
                              ps[:, TB0 + b, :].rearrange("p (t c) -> p t c", t=4),
                              xgT_hi[:, 4 * q:4 * q + 4, :].bitcast(FP32), ALU.subtract)\
               .then_inc(tb_free[b], 1)

        def step(n, e, last_step):
            for j in range(LEAD, ECH + (0 if last_step else LEAD)):
                if j == 3 and not last_step:
                    place(n + 1)
                expert_lo(dve, n, j)
                if j == 3 and not last_step:
                    rows(n + 1)
                if j in (8, 10):
                    h = (j - 8) // 2
                    col = slice(FH * h, FH * (h + 1))
                    dve.wait_ge(w_used, CHUNKS1 + 6 + 2 * h + n * ECH)
                    if h == 0:
                        dve.wait_ge(silu_ready, n + 1)
                        dve.wait_ge(rows_ready, n + 1)
                    dve.scalar_tensor_tensor(out=a_sb[:, col], in0=ps[:, HALF[h], 0:FH],
                                             scalar=gates[:, bass.ds(n, 1)], in1=silu[:, col],
                                             op0=ALU.mult, op1=ALU.mult).then_inc(a_ready, 1)
                if j in (9, 11):
                    h = (j - 9) // 2
                    dve.wait_ge(aT_hi_ready, 2 * n + h + 1)
                    dve.tensor_tensor(aT_lo[:, 2 * h:2 * h + 2, :],
                                      ps[:, HALF[h], 0:FH].rearrange("p (t c) -> p t c", t=2),
                                      aT_hi[:, 2 * h:2 * h + 2, :].bitcast(FP32), ALU.subtract)\
                       .then_inc(aT_lo_ready, 1)
                if j >= 11 and not last_step:
                    tokens_lo(n + 1, j - 11)

        def one_round(r):
            n = r * NE
            place(n)
            rows(n)
            if not isinstance(r, int):
                for j in range(LEAD):
                    expert_lo(dve, n, j)
            for q in range(4):
                tokens_lo(n, q)
            each_expert(dve, r, step)

        each_round(dve, one_round)

    def dve_finish(dve):
        steps = Tally(fin_step)

        def link(instruction):
            dve.wait_ge(fin_step, steps.inc(instruction))

        for i, (t0, m) in enumerate(TILES):
            dve.wait_ge(fin_in[i], 16)
            a, b = yrows[i][0:m, 0, :], yrows[i][0:m, 1, :]
            x = tok[0:m, i, :]
            link(dve.tensor_tensor(a, a, b, ALU.add))
            link(dve.scalar_tensor_tensor(out=x, in0=x, scalar=ALPHA, in1=a, op0=ALU.mult, op1=ALU.add))
            for q in range(4):
                link(dve.bn_stats(xstats[0:m, i, q, :], tok[0:m, i, 512 * q:512 * (q + 1)]))
            link(dve.bn_aggr(vmv[0:m, i, :], xstats[0:m, i, 0:4, :].rearrange("p a b -> p (a b)")))
            dve.tensor_scalar(vstd[:, i:i + 1], vmv[:, i, 1:2], EPS, None, ALU.add).then_inc(fin_sum, 1)
            dve.wait_ge(fin_std, i + 1)
            link(dve.reciprocal(vrstd[:, i:i + 1], vrstd[:, i:i + 1]))
            dve.wait_ge(ln2_in, 32)
            link(dve.scalar_tensor_tensor(out=x, in0=x, scalar=vmv[0:m, i, 0:1], in1=lng[0:m, :],
                                          op0=ALU.subtract, op1=ALU.mult))
            dve.scalar_tensor_tensor(out=x, in0=x, scalar=vrstd[0:m, i:i + 1], in1=lnb[0:m, :],
                                     op0=ALU.mult, op1=ALU.add).then_inc(fin_ready, 1)

    with nc.Block() as block:
        @block.sync
        def _(sp):
            sp_program(sp)
            sp_experts(sp)
            sp_finish(sp)

        @block.gpsimd
        def _(pool):
            pool_program(pool)
            pool_experts(pool)

        @block.scalar
        def _(act):
            act_mixer(act)
            act_router(act)
            act_experts(act)
            act_finish(act)

        @block.tensor
        def _(pe):
            pe_mixer(pe)
            pe_router(pe)
            pe_experts(pe)

        @block.vector
        def _(dve):
            steps, link = dve_mixer(dve)
            dve_router(dve, steps, link)
            dve_experts(dve)
            dve_finish(dve)


_INS = ["x_prompt", "x_sample", "state_conv", "state_pool", "w_in", "conv_w", "sgu_ln_g", "sgu_ln_b",
        "sgu_w", "sgu_b", "pool_w", "pool_scale", "w_out", "ln1_g", "ln1_b", "router_group_w",
        "router_group_b", "router_expert_w", "router_expert_b", "expert_w_gate", "expert_w_up",
        "expert_w_down", "ln2_g", "ln2_b"]


def kernel(**inputs):
    import numpy as np
    import concourse.bacc as bacc
    from concourse import mybir as mb
    from concourse.bass_utils import run_bass_kernel_spmd

    nc = bacc.Bacc("TRN2", target_bir_lowering=False, num_devices=1)
    arrays, args = {}, []
    for name in _INS:
        a = np.ascontiguousarray(inputs[name])
        arrays[f"in_{name}"] = a
        args.append(nc.dram_tensor(f"in_{name}", a.shape, mb.dt.from_np(a.dtype),
                                   kind="ExternalInput").ap())
    b, s, d = inputs["x_prompt"].shape
    nb, nt = inputs["x_sample"].shape[0:2]
    depth, _, rows, conv = inputs["state_conv"].shape
    prows, pool = inputs["state_pool"].shape[2:4]
    chunk = inputs["sgu_ln_g"].shape[1]
    outs = [(b, s, d), (nb, nt, d), (depth, b, rows, conv), (depth, b, prows, pool),
            (depth, nb, rows, conv), (depth, nb, prows, pool), (depth, nb, nt, chunk)]
    for i, shape in enumerate(outs):
        args.append(nc.dram_tensor(f"out_{i}", shape, mb.dt.float32, kind="ExternalOutput").ap())
    hybrid_trunk_kernel(nc, *args)
    r = run_bass_kernel_spmd(nc, [arrays], core_ids=[0])
    return tuple(np.asarray(r.results[0][f"out_{i}"]).reshape(shape) for i, shape in enumerate(outs))
```

```python
import concourse.bass as bass
from concourse import mybir

FP32 = mybir.dt.float32
F32R = mybir.dt.float32r
INT32 = mybir.dt.int32
ALU = mybir.AluOpType
ACT = mybir.ActivationFunctionType
AXX = mybir.AxisListType.X

P = 128
ALPHA = 2 ** 0.25
EPS = 1e-5


class Tally:

    def __init__(self, sem):
        self.sem, self.value, self.base, self.per = sem, 0, 0, None

    def inc(self, instruction):
        instruction.then_inc(self.sem, 1)
        self.value = self.value + 1
        self.base += 1
        return self.value

    def enter(self, turn, per):
        self.start, self.per = self.base, per
        self.value = self.base + turn * per

    def leave(self, turns):
        assert self.base - self.start == self.per, (self.base - self.start, self.per)
        self.base = self.value = self.start + self.per * turns


def hybrid_trunk_kernel(nc, x_prompt, x_sample, state_conv, state_pool, w_in, conv_w, sgu_ln_g,
                        sgu_ln_b, sgu_w, sgu_b, pool_w, pool_scale, w_out, ln1_g, ln1_b,
                        rg_w, rg_b, re_w, re_b, w_gate, w_up, w_down, ln2_g, ln2_b,
                        y_prompt, y_sample, new_conv_prompt, new_pool_prompt, new_conv_sample,
                        new_pool_sample, new_chunk_v):
    D = x_prompt.shape[2]
    SEQ = x_prompt.shape[1]
    NB, NT = x_sample.shape[0:2]
    NTOK = SEQ + NB * NT
    TILES = [(0, P), (P, P), (SEQ, NTOK - SEQ)]
    KT = D // P
    CONV = state_conv.shape[3]
    POOL = state_pool.shape[3]
    CHW = D - CONV - POOL
    CT, HT, PT = CONV // P, CHW // P, POOL // P
    PBUF = state_pool.shape[2]
    NG, NE = rg_w.shape[2], re_w.shape[2]
    EG = NE // NG
    F = w_gate.shape[3]
    FT = F // P

    GW = 2 * P
    CK = 8
    CH = CK * GW
    RING = 3
    G_P, G_V, G_U, G_H, G_C, G_B, G_O = 0, 2, 5, 8, 11, 14, 17
    G_END = G_O + D // GW
    CHUNKS1 = 2 * G_END
    TB0 = 6

    uses = [f"x{i}{q}" for i in range(3) for q in range(4)]
    uses += ["par", "spool", "sconv"]
    uses += [f"pool{g}" for g in range(PT)] + ["pout0", "pout1", "ws0", "ws1", "wsb"]
    uses += [f"v{i}{q}" for i in range(3) for q in range(2)]
    uses += [f"mix{h}" for h in range(HT)] + ["z0", "z1"]
    USE = {name: n for n, name in enumerate(uses)}
    USE_O = len(uses)
    USE_R = USE_O + 2 * (G_END - G_O)
    uses = ["bias"] + [f"r{i}{q}" for i in range(3) for q in range(4)] + ["lgT", "lg", "pos"]
    USE.update({name: USE_R + n for n, name in enumerate(uses)})
    USE_E = USE_R + len(uses)

    C = 68
    ROUNDS = -(-NTOK // C)
    STEPS = ROUNDS * NE
    ECH = 12
    LEAD = 6
    BIG = 4096.0

    KB = 1024
    base = (nc.sbuf_base + 63) // 64 * 64

    def at(name, offset, shape, dt=FP32):
        return nc.alloc_sbuf_tensor_at(name, shape, dt, offset=base + offset, align_bytes=4)

    RAW0 = 0
    RING_HI = RAW0 + 6 * 8 * KB
    RING_LO = RING_HI + 24 * KB
    TOK0 = RING_LO + 24 * KB
    XA = TOK0 + 24 * KB
    XT_B = KT * NTOK * 4
    YT_HI0, YT_LO0 = XA + 2 * XT_B, XA + 3 * XT_B
    MISC = XA + 4 * XT_B
    raw = [at(f"raw{s}", RAW0 + s * 8 * KB, [P, CH]) for s in range(6)]
    w_hi = [at(f"w_hi{s}", RING_HI + s * 8 * KB, [P, CH], F32R) for s in range(RING)]
    w_lo = [at(f"w_lo{s}", RING_LO + s * 8 * KB, [P, CH], F32R) for s in range(RING)]
    tok = at("tok", TOK0, [P, 3, D])
    brow = at("brow", TOK0, [P, 3, D])[64:65, 2, 0:HT * P].rearrange("p (h c) -> p h c", h=HT)
    xT_hi = at("xT_hi", XA, [P, KT, NTOK], F32R)
    xT_lo = at("xT_lo", XA + XT_B, [P, KT, NTOK], F32R)
    yT_hi = at("yT_hi", YT_HI0, [P, KT, NTOK], F32R)
    yT_lo = at("yT_lo", YT_LO0, [P, KT, NTOK], F32R)
    ROW = NTOK * 4
    T0 = RAW0 + 24 * KB
    ZW = 2 + SEQ + NB * (2 + NT)
    PW = PBUF + SEQ + NB * (PBUF + NT)
    zext = at("zext", T0, [P, CT, ZW])
    convt = at("convt", T0 + CT * ZW * 4, [P, CT, NTOK])
    PX0 = T0 + CT * ZW * 4 + CT * ROW
    pext = at("pext", PX0, [P, PT, PW])
    PX1 = PX0 + PT * PW * 4
    zstate = at("zstate", PX1, [P, CT, 2 * NB])
    zlast = at("zlast", PX1 + CT * 2 * NB * 4, [P, CT, 2 + 2 * NB])
    sum_a = at("sum_a", T0, [P, PT, PW])
    sum_b = at("sum_b", T0 + PT * PW * 4, [P, PT, PW])
    vtok = at("vtok", T0, [P, 3, CHW])
    wsT = at("wsT", PX0, [P, HT, P])
    wsbT = at("wsbT", PX0 + HT * P * 4, [64, HT, 64])
    p_out = at("p_out", T0 + 9216, [16, PT * P])
    ws_nat = at("ws_nat", YT_HI0, [P, HT, P])
    wsb_nat = at("wsb_nat", YT_HI0 + HT * P * 4, [64, HT, 64])
    sconv_nat = at("sconv_nat", YT_HI0 + HT * (P + 64) * 4, [2 * NB, CONV])
    spool_nat = at("spool_nat", YT_HI0 + 12 * ROW, [NB * PBUF, POOL])
    poolw = at("poolw", YT_HI0 + 12 * ROW + POOL * 4, [P, PT, P])
    vT = at("vT", YT_HI0 + 6 * ROW, [P, HT, NTOK])
    pdiff = at("pdiff", YT_LO0, [P, PT, NTOK])
    pnew = at("pnew", YT_LO0 + 4 * ROW, [P, PT, NB * NT])
    mixu = at("mixu", YT_LO0, [P, HT, NTOK])
    sg_g = at("sg_g", YT_LO0 + 6 * ROW, [P, CHW])
    sg_b = at("sg_b", YT_LO0 + 6 * ROW + CHW * 4, [P, CHW])
    z_out = at("z_out", PX0, [2 + 2 * NB, CONV])
    p_out2 = at("p_out2", T0 + 9216 + PT * P * 4, [64, PT * P])
    par_nat = at("par_nat", PX1 + CT * (2 * NB + 2 + 2 * NB) * 4, [3 * CT + PT, P])
    lng = at("lng", XA, [P, D])
    lnb = at("lnb", XA + 8 * KB, [P, D])
    mixT = [at(f"mixT{s}", XA + 16 * KB + s * 2 * ROW, [P, 2, NTOK]) for s in range(3)]
    tmp = at("tmp", MISC, [P, PT, NTOK])
    CO = MISC + PT * ROW
    ident = at("ident", CO, [P, P])
    before = at("before", CO + 512, [P, P])
    ones = at("ones", CO + 1024, [P, P])
    slots = at("slots", CO + 1536, [P, P])
    parT = at("parT", CO + 2048, [P, 3 * CT + PT])
    rcount = at("rcount", CO + 2144, [P, 16])
    vstats = at("vstats", CO + 2208, [P, 3, 2, 6])
    vmv = at("vmv", CO + 2352, [P, 3, 2])
    vstd = at("vstd", CO + 2376, [P, 3])
    vrstd = at("vrstd", CO + 2388, [P, 3])
    rcount_i = at("rcount_i", CO + 2400, [P, 16], INT32)
    slots_i = at("slots_i", CO + 1536, [P, P], INT32)
    xstats = at("xstats", MISC, [P, 3, 8, 6])
    rg_nat = at("rg_nat", XA + 24064, [P, KT, NG])
    re_nat = at("re_nat", XA + 24320, [P, KT, NE])
    rw = at("rw", XA + 25344, [P, KT, NG + NE])
    rbias = at("rbias", XA + 26624, [1, NG + NE])
    x1T = at("x1T", XA + 26720, [P, KT, NTOK])
    rbias_all = at("rbias_all", XA + 48384, [1, NG + NE])
    yout = at("yout", XA + 16 * KB, [P, D])
    onehot = at("onehot", XA + 47232, [P, 3, C])
    xg = at("xg", XA + 48 * KB, [P, D])
    xgT_hi = at("xgT_hi", XA + 56 * KB, [P, KT, C], F32R)
    xgT_lo = at("xgT_lo", XA + 64 * KB, [P, KT, C], F32R)
    aT_hi = at("aT_hi", XA + 72 * KB, [P, FT, C], F32R)
    aT_lo = at("aT_lo", XA + 74 * KB, [P, FT, C], F32R)
    silu = at("silu", XA + 76 * KB, [P, F])
    a_sb = at("a_sb", XA + 78 * KB, [P, F])
    lgT = at("lgT", XA + 78 * KB, [NG + NE, 3 * P])
    small = [MISC + 576]

    def little(name, shape, dt=FP32):
        n = 4
        for d in shape[1:]:
            n *= d
        t = at(name, small[0], shape, dt)
        small[0] += n
        assert small[0] <= CO
        return t

    logits = little("logits", [P, 3, NG + NE])
    rank = little("rank", [P, 3, STEPS])
    facts = little("facts", [P, 3, NE, 2])
    token_i = little("token_i", [P, 3], INT32)
    token = little("token", [P, 3])
    earlier = little("earlier", [P, 4, 4])
    LG = NG + 1
    most_of = little("most_of", [P, 3 * LG])
    expd = little("expd", [P, 3, NG + NE])
    beaten = at("beaten", XA + 16 * KB, [P, 3 * LG, 4, 8])
    place_in = little("place_in", [P, 3, NG + NE])
    group_of = little("group_of", [P, 3, NG])
    mask = little("mask", [P, 3, NE])
    chosen = little("chosen", [P, 3, NE])
    gsum = little("gsum", [P, 3])
    esum = little("esum", [P, 3])
    gb_nat = little("gb_nat", [P, 2, KT])
    norm_bias = little("norm_bias", [P, 3])
    count_max = little("count_max", [P, 1])
    gather_row = little("gather_row", [P, 1], INT32)
    result_rows = little("result_rows", [P, STEPS], INT32)
    result_row = little("result_row", [P, 1], INT32)
    gates = little("gates", [P, STEPS])
    fullest = little("fullest", [P, 2], INT32)
    ps = nc.alloc_psum_tensor("ps", [P, 8, 512], FP32)

    S = nc.alloc_semaphore
    act_step = S("act_step")
    raw_full = [S(f"raw_full{s}") for s in range(6)]
    hi_ready, lo_ready = S("hi_ready"), S("lo_ready")
    w_used = S("w_used")
    x_in = [S(f"x_in{i}") for i in range(3)]
    pool_const = S("pool_const")
    par_in = S("par_in")
    sgu_in = S("sgu_in")
    state_in = S("state_in")
    tb_full = [S(f"tb_full{b}") for b in range(2)]
    tb_free = [S(f"tb_free{b}") for b in range(2)]
    xhi_ready = S("xhi_ready")
    pair_free = [S(f"pair_free{k}") for k in range(3)]
    dve_step = S("dve_step")
    yhi_ready, ylo_ready = S("yhi_ready"), S("ylo_ready")
    diff_ready, z_ready = S("diff_ready"), S("z_ready")
    var_ready, std_ready, vn_ready = S("var_ready"), S("std_ready"), S("vn_ready")
    gb_in = S("gb_in")
    small_out = S("small_out")
    copy_out = S("copy_out")
    sp_turns, pool_turns = S("sp_turns"), S("pool_turns")
    rw_in = S("rw_in")
    gb_nat_in = S("gb_nat_in")
    rw_ready = S("rw_ready")
    bias_ready = S("bias_ready")
    norm_ready = S("norm_ready")
    t_ready = [S(f"t_ready{i}") for i in range(3)]
    xg_ready = [S(f"xg_ready{i}") for i in range(3)]
    x1_ready = [S(f"x1_ready{i}") for i in range(3)]
    x1_stored = S("x1_stored")
    lgT_pad, lgT_ready, logits_ready = S("lgT_pad"), S("lgT_ready"), S("logits_ready")
    gexp_in, gexp_out = S("gexp_in"), S("gexp_out")
    mask_ready, facts_ready = S("mask_ready"), S("facts_ready")
    chosen_ready, counted = S("chosen_ready"), S("counted")
    onehot_ready = S("onehot_ready")
    slots_made, rows_ready = S("slots_made"), S("rows_ready")
    xg_zero = S("xg_zero")
    gathered, scattered = S("gathered"), S("scattered")
    silu_ready, a_ready = S("silu_ready"), S("a_ready")
    aT_full, aT_hi_ready, aT_lo_ready = S("aT_full"), S("aT_hi_ready"), S("aT_lo_ready")
    xg_hi_ready = S("xg_hi_ready")
    y_read, yout_free = S("y_read"), S("yout_free")
    result_row_ready = S("result_row_ready")
    experts_done = S("experts_done")
    fin_in = [[S(f"fin_in{i}{h}") for h in range(2)] for i in range(3)]
    ln2_in = S("ln2_in")
    fin_step, fin_std = S("fin_step"), S("fin_std")
    alpha_ready, base_stored = S("alpha_ready"), S("base_stored")
    fin_var, fin_scale = S("fin_var"), S("fin_scale")
    fin_norm, fin_gain = S("fin_norm"), S("fin_gain")
    fin_ready = [S(f"fin_ready{i}") for i in range(3)]
    y_out = S("y_out")
    x1_dram = nc.dram_tensor("x1_rows", (NTOK, D), FP32).ap()
    sum_dram = nc.dram_tensor("sum_rows", (NTOK, D), FP32).ap()

    def tb(n):
        return n % 2, n // 2 + 1

    def wait_read(eng, *names):
        for name in names:
            b, full = tb(USE[name])
            eng.wait_ge(tb_free[b], full)

    def wait_group_read(eng, g):
        eng.wait_ge(pair_free[g % 3], g // 3 + 1)


    win_v = w_in[0].rearrange("(p t) n -> p t n", t=KT)
    wout_v = w_out[0].rearrange("(j p) n -> p j n", p=P)
    COL_P, COL_V = 3 * CONV + 2 * CHW, 3 * CONV + CHW
    x_tiles = [x_prompt[0, 0:P, :], x_prompt[0, P:SEQ, :], x_sample.rearrange("b t d -> (b t) d")]

    HALF_O = (1, 0)

    def wait_alone(eng, sem, value, turns):
        eng.wait_ge(sem, value)
        eng.sem_inc(turns, 1)

    def small_inputs(sp):
        sp.dma_start(par_nat[0:3 * CT, :], conv_w[0].rearrange("k (j p) -> (k j) p", p=P))\
           .then_inc(par_in, 16)
        sp.dma_start(par_nat[3 * CT:3 * CT + PT, :], pool_scale[0].rearrange("(j p) -> j p", p=P))\
           .then_inc(par_in, 16)
        sp.dma_start(poolw[:, :, :], pool_w[0].rearrange("g c d -> c g d")).then_inc(par_in, 16)
        sp.dma_start(brow, sgu_b[0:1]).then_inc(par_in, 16)
        sp.dma_start(sconv_nat[:, :], state_conv[0].rearrange("b r c -> (b r) c")).then_inc(state_in, 16)
        sp.dma_start(spool_nat[:, :], state_pool[0].rearrange("b r c -> (b r) c")).then_inc(state_in, 16)
        sp.dma_start(ws_nat[:, :, :], sgu_w[0].rearrange("h t s -> t h s")).then_inc(sgu_in, 16)
        sp.wait_ge(pool_const, 5)
        for b in range(NB):
            sp.dma_start(wsb_nat[NT * b:NT * (b + 1), :, NT * b:NT * (b + 1)],
                          sgu_w[0][:, 0:NT, 0:NT].rearrange("h t s -> t h s")).then_inc(sgu_in, 16)
        sp.dma_start(sg_g[:, :], sgu_ln_g[0:1, :].to_broadcast([P, CHW])).then_inc(gb_in, 16)
        sp.dma_start(sg_b[:, :], sgu_ln_b[0:1, :].to_broadcast([P, CHW])).then_inc(gb_in, 16)
        sp.dma_start(new_pool_sample[0][:, 0:PBUF - NT, :], state_pool[0][:, NT:PBUF, :])\
           .then_inc(copy_out, 16)

    def sp_program(sp):
        def load_x(i):
            m = TILES[i][1]
            sp.dma_start(tok[0:m, i, :], x_tiles[i]).then_inc(x_in[i], 16)

        load_x(0)
        load_x(1)
        for c in range(4):
            if c == 1:
                load_x(2)
            if c == 3:
                small_inputs(sp)
            if c >= RING:
                sp.wait_ge(lo_ready, c - RING + 1)
            g, h = c // 2, c % 2
            sp.dma_start(raw[c % 3][:, :].rearrange("p (t n) -> p t n", t=CK),
                         win_v[:, CK * h:CK * h + CK, COL_P + GW * g:COL_P + GW * (g + 1)])\
              .then_inc(raw_full[c % 3], 16)
        with sp.Fori(0, 5) as s:
            for i in range(6):
                c = 2 * G_V + 6 * s + i
                wait_alone(sp, lo_ready, c - RING + 1, sp_turns)
                k = (2 * G_V + i) % 3
                col = COL_V - CONV * s + GW * (i // 2)
                sp.dma_start(raw[k][:, :].rearrange("p (t n) -> p t n", t=CK),
                             win_v[:, CK * (i % 2):CK * (i % 2) + CK, bass.ds(col, GW)])\
                  .then_inc(raw_full[k], 16)

        def out_chunk(c, k, h, col):
            wait_alone(sp, lo_ready, c - RING + 1, sp_turns)
            sp.dma_start(raw[k][:, :].rearrange("p (t n) -> p t n", t=CK),
                         wout_v[:, CK * h:CK * h + CK, col]).then_inc(raw_full[k], 16)

        with sp.Fori(0, 2) as s:
            for i in range(6):
                out_chunk(2 * G_O + 6 * s + i, (2 * G_O + i) % 3, HALF_O[i % 2],
                          bass.ds(s * 3 * GW + GW * (i // 2), GW))
        for i in range(12, 16):
            out_chunk(2 * G_O + i, (2 * G_O + i) % 3, HALF_O[i % 2],
                      slice(GW * (i // 2), GW * (i // 2 + 1)))

    def pool_program(pool):
        pool.memset(ident[:, :], 0.0).then_inc(pool_const, 1)
        pool.memset(ones[:, :], 1.0).then_inc(pool_const, 1)
        pool.iota(slots_i[:, :], [[1, P]], base=1, channel_multiplier=0).then_inc(pool_const, 1)
        pool.iota(rcount_i[:, :], [[1, 16]], base=1, channel_multiplier=0).then_inc(pool_const, 1)
        pool.memset(wsb_nat[:, :, :], 0.0).then_inc(pool_const, 1)
        pool.wait_ge(pool_const, 5)
        pool.affine_select(out=ident[:, :], in_=ident[:, :], compare_op=ALU.not_equal, fill=1.0,
                           base=0, pattern=[[-1, P]], channel_multiplier=1).then_inc(pool_const, 1)
        pool.affine_select(out=before[:, :], in_=ones[:, :], compare_op=ALU.is_gt, fill=0.0,
                           base=0, pattern=[[1, P]], channel_multiplier=-1).then_inc(pool_const, 1)
        pool.tensor_copy(slots[:, :], slots_i[:, :]).then_inc(pool_const, 1)
        pool.tensor_copy(rcount[:, :], rcount_i[:, :]).then_inc(pool_const, 1)
        pool.wait_ge(sgu_in, 16 * (1 + NB))
        pool.affine_select(out=ws_nat[:, :, :], in_=ws_nat[:, :, :], compare_op=ALU.is_ge, fill=0.0,
                           base=0, pattern=[[0, HT], [-1, P]], channel_multiplier=1)\
            .then_inc(pool_const, 1)
        pool.affine_select(out=wsb_nat[:, :, :], in_=wsb_nat[:, :, :], compare_op=ALU.is_ge,
                           fill=0.0, base=0, pattern=[[0, HT], [-1, NB * NT]],
                           channel_multiplier=1).then_inc(pool_const, 1)

    def group_products(pe, g, acts, halves, turn=0, turns_at=0, wait_half=None):
        hi, lo = acts
        pair = g % 3
        if g >= 3:
            pe.wait_ge(pair_free[pair], g // 3 + turn * (turns_at // 3))
        for n in range(2):
            if n and wait_half:
                pe.wait_ge(*wait_half)
            k = (2 * g + n) % 3
            pe.wait_ge(lo_ready, 2 * g + n + 1 + turn * (2 * turns_at))
            wh = w_hi[k][:, :].rearrange("p (t n) -> p t n", t=CK)
            wl = w_lo[k][:, :].rearrange("p (t n) -> p t n", t=CK)
            for t in range(CK):
                kt = CK * halves[n] + t
                for f in range(2):
                    out = ps[:, 2 * pair + f, 0:NTOK]
                    col = slice(P * f, P * (f + 1))
                    pe.matmul(out, wh[:, t, col], hi[:, kt, :], start=(n == 0 and t == 0), stop=False)
                    pe.matmul(out, wh[:, t, col], lo[:, kt, :], start=False, stop=False)
                    last = pe.matmul(out, wl[:, t, col], hi[:, kt, :], start=False,
                                     stop=(n == 1 and t == CK - 1))
            last.then_inc(w_used, 1)

    def pe_mixer(pe):
        def bank_of(n, add=0):
            b, full = tb(n)
            if n >= 2:
                pe.wait_ge(tb_free[b], full - 1 + add)
            return b, ps[:, TB0 + b, :]

        pe.wait_ge(pool_const, 6)
        for i, (t0, m) in enumerate(TILES):
            pe.wait_ge(x_in[i], 16)
            for q in range(4):
                b, bank = bank_of(USE[f"x{i}{q}"])
                for t in range(4):
                    last = pe.transpose(bank[:, P * t:P * t + m], tok[0:m, i, 4 * q + t::KT],
                                        ident[0:m, 0:m])
                last.then_inc(tb_full[b], 1)
        X, Y = (xT_hi, xT_lo), (yT_hi, yT_lo)
        wait_read(pe, "x22", "x23")
        group_products(pe, 0, X, (0, 1))
        group_products(pe, 1, X, (0, 1))
        pe.wait_ge(par_in, 16 * 4)
        b, bank = bank_of(USE["par"])
        n = 3 * CT + PT
        pe.transpose(bank[:, 0:n], par_nat[:, :], ident[0:n, 0:n]).then_inc(tb_full[b], 1)
        pe.wait_ge(state_in, 32)
        b, bank = bank_of(USE["spool"])
        for j in range(PT):
            last = pe.transpose(bank[:, P * j:P * j + NB * PBUF], spool_nat[:, P * j:P * (j + 1)],
                                ident[0:NB * PBUF, 0:NB * PBUF])
        last.then_inc(tb_full[b], 1)
        b, bank = bank_of(USE["sconv"])
        for j in range(CT):
            last = pe.transpose(bank[:, 2 * NB * j:2 * NB * (j + 1)], sconv_nat[:, P * j:P * (j + 1)],
                                ident[0:2 * NB, 0:2 * NB])
        last.then_inc(tb_full[b], 1)
        group_products(pe, 2, X, (0, 1))
        pe.wait_ge(diff_ready, 1)
        for j in range(PT):
            b, bank = bank_of(USE[f"pool{j}"])
            pe.matmul(bank[:, 0:NTOK], poolw[:, j, :], pdiff[:, j, :], start=True, stop=True)\
              .then_inc(tb_full[b], 1)
        b, bank = bank_of(USE["pout0"])
        for j in range(PT):
            last = pe.transpose(bank[0:16, P * j:P * (j + 1)], pext[:, j, PBUF + SEQ - 16:PBUF + SEQ],
                                ident[:, :])
        last.then_inc(tb_full[b], 1)
        b, bank = bank_of(USE["pout1"])
        for j in range(PT):
            last = pe.transpose(bank[0:64, P * j:P * (j + 1)], pnew[:, j, :], ident[:, :])
        last.then_inc(tb_full[b], 1)
        group_products(pe, 3, X, (0, 1))
        pe.wait_ge(pool_const, 11)
        for n, heads in enumerate((range(0, 4), range(4, HT))):
            b, bank = bank_of(USE[f"ws{n}"])
            for h in heads:
                last = pe.transpose(bank[:, P * (h % 4):P * (h % 4) + P], ws_nat[:, h, :], ident[:, :])
            last.then_inc(tb_full[b], 1)
        b, bank = bank_of(USE["wsb"])
        for h in range(HT):
            last = pe.transpose(bank[0:64, 64 * h:64 * (h + 1)], wsb_nat[:, h, :], ident[0:64, 0:64])
        last.then_inc(tb_full[b], 1)
        group_products(pe, 4, X, (0, 1))
        group_products(pe, 5, X, (0, 1))
        wait_group_read(pe, G_V + 2)
        for i, (t0, m) in enumerate(TILES):
            for q, heads in enumerate((range(0, 4), range(4, HT))):
                b, bank = bank_of(USE[f"v{i}{q}"])
                for h in heads:
                    last = pe.transpose(bank[0:m, P * (h % 4):P * (h % 4) + P], vT[:, h, t0:t0 + m],
                                        ident[:, :])
                last.then_inc(tb_full[b], 1)
        group_products(pe, 6, X, (0, 1))
        pe.wait_ge(vn_ready, 3)
        for h in range(HT):
            b, bank = bank_of(USE[f"mix{h}"])
            one = ones[64:65, :]
            head = slice(P * h, P * (h + 1))
            for c in range(2):
                out = bank[:, P * c:P * (c + 1)]
                pe.matmul(out, vtok[:, c, head], wsT[:, h, :], start=True, stop=False)
                pe.matmul(out, one, brow[:, h, :], start=False, stop=True)
            out = bank[:, SEQ:NTOK]
            pe.matmul(out, vtok[0:64, 2, head], wsbT[:, h, :], start=True, stop=False)
            pe.matmul(out.rearrange("p (b t) -> p b t", b=NB), one,
                      brow[:, h:h + 1, 0:NT].to_broadcast([1, NB, NT]),
                      start=False, stop=True).then_inc(tb_full[b], 1)
        group_products(pe, 7, X, (0, 1))
        with pe.Fori(0, 3) as s:
            for i in range(3):
                group_products(pe, G_H + i, X, (0, 1), s, 3)
        pe.wait_ge(z_ready, 1)
        for n, tiles in enumerate((range(0, 4), range(4, CT))):
            b, bank = bank_of(USE[f"z{n}"])
            for j in tiles:
                last = pe.transpose(bank[0:2 + 2 * NB, P * (j % 4):P * (j % 4) + P], zlast[:, j, :],
                                    ident[:, :])
            last.then_inc(tb_full[b], 1)

        def out_tokens(k, turn=0):
            wait = pair_free[(G_O + k) % 3], (G_O + k) // 3 + 1 + turn
            pe.wait_ge(*wait)
            buf = mixT[k % 3]
            n = USE_O + 2 * k
            b, bank = bank_of(n, 3 * turn)
            b2, bank2 = bank_of(n + 1, 3 * turn)
            for i in range(2):
                for f in range(2):
                    last = pe.transpose(bank[:, GW * i + P * f:GW * i + P * (f + 1)],
                                        buf[:, f, P * i:P * (i + 1)], ident[:, :])
            last.then_inc(tb_full[b], 1)
            b, bank = b2, bank2
            for f in range(2):
                last = pe.transpose(bank[0:64, P * f:P * (f + 1)], buf[:, f, SEQ:NTOK], ident[:, :])
            last.then_inc(tb_full[b], 1)

        pe.wait_ge(ylo_ready, 4)
        group_products(pe, G_O, Y, HALF_O, wait_half=(ylo_ready, 7))
        with pe.Fori(0, 2) as s:
            for i in range(3):
                group_products(pe, G_O + 1 + i, Y, HALF_O, s, 3)
                out_tokens(i, s)
        group_products(pe, G_END - 1, Y, HALF_O)
        out_tokens(6)
        out_tokens(7)

    def split_hi(act, c, turn=0, per=0):
        k = c % 3
        act.wait_ge(raw_full[k], 16 * (c // 3 + 1) + turn * (16 * per // 3))
        if c >= RING:
            act.wait_ge(w_used, c - RING + 1 + turn * per)
        act.activation(w_hi[k][:, :], raw[k][:, :], ACT.Copy).then_inc(hi_ready, 1)

    def split_lo(dve, c, turn=0, per=0):
        k = c % 3
        dve.wait_ge(hi_ready, c + 1 + turn * per)
        dve.tensor_tensor(w_lo[k][:, :], raw[k][:, :], w_hi[k][:, :].bitcast(FP32), ALU.subtract)\
           .then_inc(lo_ready, 1)

    def act_mixer(act):
        def copy_use(name, out, in_of):
            b, full = tb(USE[name])
            act.wait_ge(tb_full[b], full)
            act.activation(out, in_of(ps[:, TB0 + b, :]), ACT.Copy).then_inc(tb_free[b], 1)

        def copy_group(g, out):
            pair = g % 3
            act.wait_ge(w_used, 2 * g + 2)
            act.activation(out, ps[:, 2 * pair:2 * pair + 2, 0:NTOK], ACT.Copy)\
               .then_inc(pair_free[pair], 1)

        def y_hi(first, n):
            act.activation(yT_hi[:, first:first + n, :], tmp[:, 0:n, :], ACT.Copy).then_inc(yhi_ready, 1)

        for i, (t0, m) in enumerate(TILES):
            for q in range(4):
                if (i, q) == (1, 2):
                    split_hi(act, 0)
                b, full = tb(USE[f"x{i}{q}"])
                act.wait_ge(tb_full[b], full)
                act.activation(xT_hi[:, 4 * q:4 * q + 4, t0:t0 + m],
                               ps[:, TB0 + b, :].rearrange("p (t c) -> p t c", t=4)[:, :, 0:m],
                               ACT.Copy).then_inc(xhi_ready, 1)

        def sample_new(g2, width, hist):
            return g2.rearrange("p j (b t) -> p j b t", b=NB)[:, :, :, hist:hist + NT]

        for g in range(G_O + 1):
            if g > 0:
                split_hi(act, 2 * g)
            split_hi(act, 2 * g + 1)
            if g in (1, 2):
                k = g - 1
                act.wait_ge(w_used, 2 * k + 2)
                if k == 0:
                    act.wait_ge(dve_step, 1)
                bank2 = ps[:, 2 * k:2 * k + 2, :]
                act.activation(pext[:, 2 * k:2 * k + 2, PBUF:PBUF + SEQ], bank2[:, :, 0:SEQ], ACT.Copy)\
                   .then_inc(act_step, 1)
                act.activation(pnew[:, 2 * k:2 * k + 2, :], bank2[:, :, SEQ:NTOK], ACT.Copy)\
                   .then_inc(act_step, 1)
                for f in range(2):
                    out = pext[:, 2 * k + f, PBUF + SEQ:PW].rearrange("p (b t) -> p b t", b=NB)
                    last = act.activation(out[:, :, PBUF:PBUF + NT],
                                          ps[:, 2 * k + f, SEQ:NTOK].rearrange("p (b t) -> p b t", b=NB),
                                          ACT.Copy)
                    last.then_inc(pair_free[k] if f else act_step, 1)
            if g == 2:
                copy_use("par", parT[:, :], lambda bank: bank[:, 0:3 * CT + PT])
                for j in range(PT):
                    b, full = tb(USE["spool"])
                    act.wait_ge(tb_full[b], full)
                    out = pext[:, j, PBUF + SEQ:PW].rearrange("p (b t) -> p b t", b=NB)
                    act.activation(out[:, :, 0:PBUF],
                                   ps[:, TB0 + b, P * j:P * j + NB * PBUF].rearrange("p (b t) -> p b t", b=NB),
                                   ACT.Copy).then_inc(tb_free[b] if j == PT - 1 else act_step, 1)
                copy_use("sconv", zstate[:, :, :],
                         lambda bank: bank[:, 0:CT * 2 * NB].rearrange("p (j c) -> p j c", j=CT))
            if g == 3:
                wait_read(act, f"pool{PT - 2}", f"pool{PT - 1}")
                y_hi(12, PT)
                copy_use("pout0", p_out[:, :], lambda bank: bank[0:16, :])
                copy_use("pout1", p_out2[:, :], lambda bank: bank[0:64, :])
                wait_read(act, "pout0", "pout1")
                act.dma_start(new_pool_prompt[0, 0], p_out[1:16, :]).then_inc(small_out, 16)
                for b in range(NB):
                    act.dma_start(new_pool_sample[0, b, PBUF - NT:PBUF, :],
                                  p_out2[NT * b:NT * (b + 1), :]).then_inc(small_out, 16)
                copy_group(G_V, vT[:, 0:2, :])
            if g == 4:
                copy_use("ws0", wsT[:, 0:4, :], lambda bank: bank.rearrange("p (h c) -> p h c", h=4))
                copy_use("ws1", wsT[:, 4:HT, :],
                         lambda bank: bank[:, 0:(HT - 4) * P].rearrange("p (h c) -> p h c", h=HT - 4))
                copy_use("wsb", wsbT[:, :, :],
                         lambda bank: bank[0:64, 0:HT * 64].rearrange("p (h c) -> p h c", h=HT))
                copy_group(G_V + 1, vT[:, 2:4, :])
            if g == 5:
                copy_group(G_V + 2, vT[:, 4:6, :])
            if g == 6:
                for i, (t0, m) in enumerate(TILES):
                    copy_use(f"v{i}0", vtok[0:m, i, 0:4 * P], lambda bank: bank[0:m, :])
                    copy_use(f"v{i}1", vtok[0:m, i, 4 * P:CHW], lambda bank: bank[0:m, 0:CHW - 4 * P])
                act.wait_ge(var_ready, 1)
                act.activation(vrstd[:, :], vstd[:, :], ACT.Sqrt).then_inc(std_ready, 1)
            if g == 7:
                act.wait_ge(vn_ready, 3)
                act.dma_start(new_chunk_v[0].rearrange("b t c -> (b t) c"), vtok[0:64, 2, :])\
                   .then_inc(small_out, 16)
                for h in range(HT):
                    copy_use(f"mix{h}", mixu[:, h, :], lambda bank: bank[:, 0:NTOK])
            if g in (7, 8, 9):
                wait_group_read(act, g - 2)
                y_hi(6 + 2 * (g - 7), 2)
            if g == 10:
                act.wait_ge(small_out, 16 * (2 + NB))
            if g in (10, 11, 12):
                copy_group(g - 2, convt[:, 2 * (g - 10):2 * (g - 10) + 2, :])
            if g in (16, 17):
                wait_group_read(act, g - 2)
                y_hi(2 * (g - 16), 2)
            if g == 17:
                wait_group_read(act, g - 1)
                y_hi(4, 2)
                copy_use("z0", z_out[:, 0:4 * P], lambda bank: bank[0:2 + 2 * NB, :])
                copy_use("z1", z_out[:, 4 * P:CONV], lambda bank: bank[0:2 + 2 * NB, 0:CONV - 4 * P])
                wait_read(act, "z0", "z1")
                act.dma_start(new_conv_prompt[0, 0], z_out[0:2, :]).then_inc(small_out, 16)
                act.dma_start(new_conv_sample[0].rearrange("b r c -> (b r) c"), z_out[2:2 + 2 * NB, :])\
                   .then_inc(small_out, 16)
                act.dma_start(lng[:, :], ln1_g[0:1, :].to_broadcast([P, D])).then_inc(gb_in, 16)
                act.dma_start(lnb[:, :], ln1_b[0:1, :].to_broadcast([P, D])).then_inc(gb_in, 16)
                act.dma_start(rg_nat[:, :, :], rg_w[0].rearrange("(p t) n -> p t n", t=KT)).then_inc(rw_in, 16)
                act.dma_start(re_nat[:, :, :], re_w[0].rearrange("(p t) n -> p t n", t=KT)).then_inc(rw_in, 16)
                act.dma_start(rbias[:, 0:NG], rg_b[0:1, :]).then_inc(rw_in, 16)
                act.dma_start(rbias[:, NG:NG + NE], re_b[0:1, :]).then_inc(rw_in, 16)

        def copy_out_group(k, turn=0):
            g = G_O + k
            pair = g % 3
            act.wait_ge(w_used, 2 * g + 2 + 6 * turn)
            if k >= 3 or not isinstance(turn, int):
                b, full = tb(USE_O + 2 * k + 1)
                act.wait_ge(tb_full[b], full - 3 + 3 * turn)
            act.activation(mixT[k % 3][:, :, :], ps[:, 2 * pair:2 * pair + 2, 0:NTOK], ACT.Copy)\
               .then_inc(pair_free[pair], 1)

        with act.Fori(0, 2) as s:
            for i in range(3):
                split_hi(act, 2 * (G_O + 1 + i), s, 6)
                split_hi(act, 2 * (G_O + 1 + i) + 1, s, 6)
                copy_out_group(i, s)
        split_hi(act, 2 * G_END - 2)
        split_hi(act, 2 * G_END - 1)
        copy_out_group(6)
        copy_out_group(7)
        act.wait_ge(var_ready, 2)
        act.activation(vrstd[:, :], vstd[:, :], ACT.Sqrt).then_inc(std_ready, 1)

    def dve_mixer(dve):
        steps = Tally(dve_step)

        def link(instruction):
            dve.wait_ge(dve_step, steps.inc(instruction))

        def y_lo(first, n, count):
            dve.wait_ge(yhi_ready, count)
            dve.tensor_tensor(yT_lo[:, first:first + n, :], tmp[:, 0:n, :],
                              yT_hi[:, first:first + n, :].bitcast(FP32), ALU.subtract)\
               .then_inc(ylo_ready, 1)
            dve.wait_ge(ylo_ready, count)

        def norm_scale():
            dve.tensor_scalar(vstd[:, :], vmv[:, :, 1], EPS, None, ALU.add).then_inc(var_ready, 1)

        link(dve.memset(pext[:, :, :], 0.0))
        link(dve.memset(vmv[:, :, :], 1.0))
        dve.wait_ge(pool_const, 9)
        link(dve.reciprocal(rcount[:, :], rcount[:, :]))
        for i, (t0, m) in enumerate(TILES):
            for q in range(4):
                if (i, q) == (1, 2):
                    split_lo(dve, 0)
                b, full = tb(USE[f"x{i}{q}"])
                dve.wait_ge(xhi_ready, 4 * i + q + 1)
                dve.tensor_tensor(xT_lo[:, 4 * q:4 * q + 4, t0:t0 + m],
                                  ps[:, TB0 + b, :].rearrange("p (t c) -> p t c", t=4)[:, :, 0:m],
                                  xT_hi[:, 4 * q:4 * q + 4, t0:t0 + m].bitcast(FP32), ALU.subtract)\
                   .then_inc(tb_free[b], 1)

        def samples(t, j, hist):
            return t[:, j, hist + SEQ:].rearrange("p (b t) -> p b t", b=NB)

        def new(t):
            return t[:, SEQ:NTOK].rearrange("p (b t) -> p b t", b=NB)

        for g in range(G_O + 2):
            if g > 0:
                split_lo(dve, 2 * g)
            split_lo(dve, 2 * g + 1)
            if g == 2:
                wait_read(dve, "spool")
                wait_group_read(dve, 1)
                wait_group_read(dve, 0)
                src, w = pext, 1
                for n, dst in enumerate((sum_a, sum_b, sum_a, sum_b)):
                    lo_ = 2 * w - 1
                    link(dve.tensor_tensor(dst[:, n:PT, lo_:PW], src[:, n:PT, lo_:PW],
                                           src[:, n:PT, lo_ - w:PW - w], ALU.add))
                    w *= 2
                    s_ = dst
                    link(dve.scalar_tensor_tensor(
                        out=pdiff[:, n, w - 1:SEQ], in0=s_[:, n, PBUF + w - 1:PBUF + SEQ],
                        scalar=1.0 / w, in1=pext[:, n, PBUF + w - 1:PBUF + SEQ],
                        op0=ALU.mult, op1=ALU.subtract))
                    link(dve.tensor_tensor(pdiff[:, n, 0:w - 1], s_[:, n, PBUF:PBUF + w - 1],
                                           rcount[:, 0:w - 1], ALU.mult))
                    link(dve.tensor_tensor(pdiff[:, n, 0:w - 1], pdiff[:, n, 0:w - 1],
                                           pext[:, n, PBUF:PBUF + w - 1], ALU.subtract))
                    last = dve.scalar_tensor_tensor(
                        out=new(pdiff[:, n, :]), in0=samples(s_, n, PBUF)[:, :, PBUF:PBUF + NT],
                        scalar=1.0 / w, in1=samples(pext, n, PBUF)[:, :, PBUF:PBUF + NT],
                        op0=ALU.mult, op1=ALU.subtract)
                    if n < PT - 1:
                        link(last)
                    else:
                        last.then_inc(diff_ready, 1)
                    src = dst
            if g == 3:
                wait_read(dve, "par")
                for j in range(PT):
                    b, full = tb(USE[f"pool{j}"])
                    dve.wait_ge(tb_full[b], full)
                    dve.tensor_scalar(tmp[:, j, :], ps[:, TB0 + b, 0:NTOK],
                                      parT[:, 3 * CT + j:3 * CT + j + 1], None, ALU.mult)\
                       .then_inc(tb_free[b], 1)
                y_lo(12, PT, 1)
            if g == 6:
                dve.wait_ge(gb_in, 32)
                for i, (t0, m) in enumerate(TILES):
                    wait_read(dve, f"v{i}0", f"v{i}1")
                    for q in range(2):
                        link(dve.bn_stats(vstats[0:m, i, q, :], vtok[0:m, i, CHW // 2 * q:CHW // 2 * (q + 1)]))
                    link(dve.bn_aggr(vmv[0:m, i, :], vstats[0:m, i, :, :].rearrange("p a b -> p (a b)")))
                norm_scale()
                dve.wait_ge(std_ready, 1)
                link(dve.reciprocal(vrstd[:, :], vrstd[:, :]))
                for i, (t0, m) in enumerate(TILES):
                    link(dve.scalar_tensor_tensor(out=vtok[0:m, i, :], in0=vtok[0:m, i, :],
                                                  scalar=vmv[0:m, i, 0:1], in1=sg_g[0:m, :],
                                                  op0=ALU.subtract, op1=ALU.mult))
                    dve.scalar_tensor_tensor(out=vtok[0:m, i, :], in0=vtok[0:m, i, :],
                                             scalar=vrstd[0:m, i:i + 1], in1=sg_b[0:m, :],
                                             op0=ALU.mult, op1=ALU.add).then_inc(vn_ready, 1)
            if g in (7, 8, 9):
                k, pair = g - 7, (g - 2) % 3
                wait_read(dve, f"mix{2 * k}", f"mix{2 * k + 1}")
                dve.wait_ge(w_used, 2 * (g - 2) + 2)
                dve.tensor_tensor(tmp[:, 0:2, :], ps[:, 2 * pair:2 * pair + 2, 0:NTOK],
                                  mixu[:, 2 * k:2 * k + 2, :], ALU.mult).then_inc(pair_free[pair], 1)
                y_lo(6 + 2 * k, 2, 2 + k)
            if g == 12:
                dve.wait_ge(small_out, 16 * (2 + NB))
                dve.wait_ge(vn_ready, 3)
                link(dve.memset(zext[:, :, 0:2], 0.0))
                for r in range(2):
                    link(dve.tensor_copy(
                        zext[:, :, 2 + SEQ:ZW].rearrange("p j (b t) -> p j b t", b=NB)[:, :, :, r],
                        zstate[:, :, :].rearrange("p j (b r) -> p j b r", b=NB)[:, :, :, r]))
            if g in (13, 14, 15):
                k, pair = g - 13, (g - 2) % 3
                wait_group_read(dve, G_H + k)
                dve.wait_ge(w_used, 2 * (g - 2) + 2)
                two = slice(2 * k, 2 * k + 2)
                link(dve.tensor_tensor(zext[:, two, 2:2 + SEQ], ps[:, 2 * pair:2 * pair + 2, 0:SEQ],
                                       convt[:, two, 0:SEQ], ALU.mult))
                for f in range(2):
                    last = dve.tensor_tensor(samples(zext, 2 * k + f, 2)[:, :, 2:2 + NT],
                                             new(ps[:, 2 * pair + f, :]), new(convt[:, 2 * k + f, :]),
                                             ALU.mult)
                    if f == 0:
                        link(last)
                last.then_inc(pair_free[pair], 1)
                wait_group_read(dve, g - 2)
                for j in (2 * k, 2 * k + 1):
                    for out, ext in ((convt[:, j, 0:SEQ], lambda r: zext[:, j, r:r + SEQ]),
                                     (new(convt[:, j, :]), lambda r: samples(zext, j, 2)[:, :, r:r + NT])):
                        link(dve.tensor_scalar(out, ext(0), parT[:, j:j + 1], None, ALU.mult))
                        for r in (1, 2):
                            link(dve.scalar_tensor_tensor(out=out, in0=ext(r),
                                                          scalar=parT[:, CT * r + j:CT * r + j + 1],
                                                          in1=out, op0=ALU.mult, op1=ALU.add))
            if g == 15:
                link(dve.tensor_copy(zlast[:, :, 0:2], zext[:, :, SEQ:SEQ + 2]))
                for r in range(2):
                    last = dve.tensor_copy(
                        zlast[:, :, 2:].rearrange("p j (b r) -> p j b r", b=NB)[:, :, :, r],
                        zext[:, :, 2 + SEQ:ZW].rearrange("p j (b t) -> p j b t", b=NB)[:, :, :, NT + r])
                    if r == 0:
                        link(last)
                last.then_inc(z_ready, 1)
            for k in {16: (0,), 17: (1, 2)}.get(g, ()):
                src = G_B + k
                pair = src % 3
                dve.wait_ge(w_used, 2 * src + 2)
                dve.tensor_tensor(tmp[:, 0:2, :], ps[:, 2 * pair:2 * pair + 2, 0:NTOK],
                                  convt[:, 2 * k:2 * k + 2, :], ALU.mult).then_inc(pair_free[pair], 1)
                y_lo(2 * k, 2, 5 + k)

        def residual(k, turn=0):
            n = USE_O + 2 * k
            col = slice(GW * k, GW * (k + 1)) if isinstance(turn, int) else \
                bass.ds(turn * (3 * GW) + GW * k, GW)
            b, full = tb(n)
            dve.wait_ge(tb_full[b], full + 3 * turn)
            dve.scalar_tensor_tensor(out=tok[:, 0:2, col], in0=tok[:, 0:2, col], scalar=ALPHA,
                                     in1=ps[:, TB0 + b, :].rearrange("p (i c) -> p i c", i=2),
                                     op0=ALU.mult, op1=ALU.add).then_inc(tb_free[b], 1)
            b2, full2 = tb(n + 1)
            dve.wait_ge(tb_full[b2], full2 + 3 * turn)
            dve.scalar_tensor_tensor(out=tok[0:64, 2, col], in0=tok[0:64, 2, col], scalar=ALPHA,
                                     in1=ps[0:64, TB0 + b2, 0:GW], op0=ALU.mult, op1=ALU.add)\
               .then_inc(tb_free[b2], 1)
            dve.wait_ge(tb_free[b], full + 3 * turn)
            dve.wait_ge(tb_free[b2], full2 + 3 * turn)
            kk = k if isinstance(turn, int) else 3 * turn + k
            for i, (t0, m) in enumerate(TILES):
                out = xstats[0:m, i, bass.ds(kk, 1), :].rearrange("p a b -> p (a b)") \
                    if not isinstance(turn, int) else xstats[0:m, i, kk, :]
                steps.inc(dve.bn_stats(out, tok[0:m, i, col]))

        with dve.Fori(0, 2) as s:
            steps.enter(s, 9)
            for i in range(3):
                split_lo(dve, 2 * (G_O + 2 + i), s, 6)
                split_lo(dve, 2 * (G_O + 2 + i) + 1, s, 6)
                residual(i, s)
        steps.leave(2)
        dve.wait_ge(rw_in, 16 * 4)
        dve.wait_ge(gb_nat_in, 16 * 2)
        gain = gb_nat[:, 0, :].unsqueeze(2)
        dve.tensor_tensor(rw[:, :, 0:NG], rg_nat[:, :, :], gain.to_broadcast([P, KT, NG]), ALU.mult)\
           .then_inc(rw_ready, 1)
        dve.tensor_tensor(rw[:, :, NG:NG + NE], re_nat[:, :, :], gain.to_broadcast([P, KT, NE]), ALU.mult)\
           .then_inc(rw_ready, 1)
        dve.wait_ge(pool_const, 14)
        steps.inc(dve.tensor_copy(facts[:, :, :, 0], token[:, :].unsqueeze(2).to_broadcast([P, 3, NE])))
        residual(6)
        residual(7)
        dve.wait_ge(dve_step, steps.value)
        for i, (t0, m) in enumerate(TILES):
            link(dve.bn_aggr(vmv[0:m, i, :], xstats[0:m, i, :, :].rearrange("p a b -> p (a b)")))
        norm_scale()
        dve.wait_ge(std_ready, 2)
        link(dve.reciprocal(vrstd[:, :], vrstd[:, :]))
        dve.scalar_tensor_tensor(out=norm_bias[:, :], in0=vmv[:, :, 0], scalar=-1.0, in1=vrstd[:, :],
                                 op0=ALU.mult, op1=ALU.mult).then_inc(norm_ready, 1)
        return steps, link

    RAW_BASE = [0, 0, 0]
    for c in range(CHUNKS1):
        RAW_BASE[c % 3] += 1

    def raw_slot(j):
        k = (j + 3) % 6
        return k, RAW_BASE[k] if k < 3 else 0

    HALVES, HRING, HC = 2 * ECH, 2 * RING, CH // 2

    def half(ring, m):
        k = (2 * CHUNKS1 + m) % HRING
        return ring[k // 2][:, HC * (k % 2):HC * (k % 2 + 1)]

    def x_use(n, q):
        b, full = tb(USE_E + q)
        return b, full + 2 * n

    def each_expert(eng, r, step):
        with eng.Fori(0, NE - 1) as e:
            step(r * NE + e, e, False)
        step(r * NE + NE - 1, NE - 1, True)

    def each_round(eng, one_round):
        one_round(0)
        eng.wait_ge(facts_ready, 1)
        most = eng.value_load(fullest[0:1, 0:1], min_val=0, max_val=NTOK)
        with eng.If(most > C):
            with eng.Fori(1, ROUNDS) as r:
                with eng.If(most > r * C):
                    one_round(r)

    gate_v = w_gate[0].rearrange("e (p t) f -> p e t f", t=KT)
    up_v = w_up[0].rearrange("e (p t) f -> p e t f", t=KT)
    down_v = w_down[0].rearrange("e (j p) d -> p e j d", p=P)
    FH = F // 2

    def sp_expert(sp, n, e, first):
        one = bass.ds(e, 1)
        for j in range(ECH):
            k, base_ = raw_slot(j)
            if first and j == 3:
                sp.wait_ge(lo_ready, CHUNKS1)
            if first and j == 6:
                for i, (t0, m) in enumerate(TILES):
                    sp.wait_ge(x1_ready[i], 1)
                    sp.dma_start(x1_dram[t0:t0 + m, :], tok[0:m, i, :]).then_inc(x1_stored, 16)
            if first and j == 9:
                sp.wait_ge(gathered, 16)
                for i, (t0, m) in enumerate(TILES):
                    sp.wait_ge(alpha_ready, i + 1)
                    sp.dma_start(sum_dram[t0:t0 + m, :], tok[0:m, i, :]).then_inc(base_stored, 16)
            wait_alone(sp, lo_ready, CHUNKS1 - 10 + 2 * j + n * HALVES, sp_turns)
            if j < 4:
                dst, src = raw[k][:, :].rearrange("p (t f) -> p t f", t=4), gate_v[:, one, 4 * j:4 * j + 4, :]
            elif j < 8:
                h, t = (j - 4) // 2, 8 * (j % 2)
                dst = raw[k][:, :].rearrange("p (t f) -> p t f", t=8)
                src = up_v[:, one, t:t + 8, FH * h:FH * (h + 1)]
            else:
                dst, src = raw[k][:, :].rearrange("p (j d) -> p j d", j=1), down_v[:, one, j - 8:j - 7, :]
            sp.dma_start(dst, src.rearrange("p e t f -> p (e t) f")).then_inc(raw_full[k], 16)

    def sp_experts(sp):
        sp.wait_ge(ylo_ready, 7)
        sp.wait_ge(small_out, 16 * (4 + NB))
        sp_expert(sp, 0, 0, True)
        with sp.Fori(1, NE) as e:
            sp_expert(sp, e, e, False)
        sp.wait_ge(facts_ready, 1)
        most = sp.value_load(fullest[0:1, 0:1], min_val=0, max_val=NTOK)
        with sp.If(most > C):
            with sp.Fori(1, ROUNDS) as r:
                with sp.If(most > r * C):
                    with sp.Fori(0, NE) as e:
                        sp_expert(sp, r * NE + e, e, False)

    def sp_finish(sp):
        sp.dma_start(lng[:, :], ln2_g[0:1, :].to_broadcast([P, D])).then_inc(ln2_in, 16)
        sp.dma_start(lnb[:, :], ln2_b[0:1, :].to_broadcast([P, D])).then_inc(ln2_in, 16)
        sp.wait_ge(experts_done, 1)
        for i, (t0, m) in enumerate(TILES):
            for h in range(2):
                col = slice(D // 2 * h, D // 2 * (h + 1))
                sp.dma_start(tok[0:m, i, col], sum_dram[t0:t0 + m, col]).then_inc(fin_in[i][h], 16)
        y_tiles = [y_prompt[0, 0:P, :], y_prompt[0, P:SEQ, :], y_sample.rearrange("b t d -> (b t) d")]
        for i, (t0, m) in enumerate(TILES):
            sp.wait_ge(fin_ready[i], 1)
            sp.dma_start(y_tiles[i], tok[0:m, i, :]).then_inc(y_out, 16)
        sp.wait_ge(y_out, 16 * 3)
        sp.wait_ge(copy_out, 16)
        sp.wait_ge(small_out, 16 * (4 + NB))

    def pool_experts(pool):
        pool.wait_ge(ylo_ready, 7)
        for k, src in enumerate((ln1_g, ln1_b)):
            pool.dma_start(gb_nat[:, k, :], src[0].rearrange("(p t) -> p t", t=KT)).then_inc(gb_nat_in, 16)
        pool.iota(token_i[:, :], [[P, 3]], base=-int(BIG), channel_multiplier=1).then_inc(pool_const, 1)
        pool.affine_select(out=earlier[:, :, :], in_=ones[:, 0:16].rearrange("p (j i) -> p j i", j=4),
                           compare_op=ALU.is_gt, fill=0.0, base=0, pattern=[[1, 4], [-1, 4]],
                           channel_multiplier=0).then_inc(pool_const, 1)
        pool.wait_ge(pool_const, 13)
        pool.tensor_copy(token[:, :], token_i[:, :]).then_inc(pool_const, 1)
        pool.wait_ge(w_used, CHUNKS1)
        pool.memset(xg[:, :], 0.0).then_inc(xg_zero, 1)
        pool.wait_ge(xg_zero, 1)
        pool.sem_inc(yout_free, 1)
        pool.memset(lgT[:, NTOK:3 * P], 0.0).then_inc(lgT_pad, 1)
        pool.wait_ge(gb_in, 64)
        for i in (0, 2):
            m = TILES[i][1]
            pool.wait_ge(xg_ready[i], 1)
            pool.tensor_tensor(tok[0:m, i, :], tok[0:m, i, :], lnb[0:m, :], ALU.add).then_inc(x1_ready[i], 1)
        pool.wait_ge(x1_stored, 16 * 3)

        def gather(n):
            wait_alone(pool, rows_ready, n + 1, pool_turns)
            pool.indirect_dma_start(
                out=xg[0:C, :], out_offset=None, in_=x1_dram,
                in_offset=bass.IndirectOffsetOnAxis(ap=gather_row[0:C, 0:1], axis=0),
                bounds_check=NTOK - 1, oob_is_err=False).then_inc(gathered, 16)

        def step(n, e, last):
            if not last:
                gather(n + 1)
            if not (isinstance(n, int) and n == 0):
                wait_alone(pool, scattered, 16 * n, pool_turns)
                pool.sem_inc(yout_free, 1)
            pool.tensor_copy(result_row[0:C, :], result_rows[0:C, bass.ds(n, 1)])\
                .then_inc(result_row_ready, 1)
            wait_alone(pool, result_row_ready, n + 1, pool_turns)
            wait_alone(pool, y_read, n + 2, pool_turns)
            if isinstance(n, int) and n == 0:
                pool.wait_ge(base_stored, 16 * 3)
            pool.indirect_dma_start(
                out=sum_dram, out_offset=bass.IndirectOffsetOnAxis(ap=result_row[0:C, 0:1], axis=0),
                in_=yout[0:C, :], in_offset=None,
                bounds_check=NTOK - 1, oob_is_err=False, compute_op=ALU.add).then_inc(scattered, 16)
            if last:
                wait_alone(pool, scattered, 16 * n + 16, pool_turns)

        def one_round(r):
            gather(r * NE)
            step(r * NE, 0, False)
            with pool.Fori(1, NE - 1) as e:
                step(r * NE + e, e, False)
            step(r * NE + NE - 1, NE - 1, True)

        each_round(pool, one_round)
        pool.sem_inc(experts_done, 1)

    def pool_finish(pool):
        pool.wait_ge(ln2_in, 32)
        for i in range(2):
            pool.wait_ge(fin_gain, i + 1)
            pool.tensor_tensor(tok[:, i, :], tok[:, i, :], lnb[:, :], ALU.add).then_inc(fin_ready[i], 1)

    COUNTS = 5

    def pe_router(pe):
        pe.wait_ge(rw_in, 16 * 4)
        pe.wait_ge(gb_nat_in, 16 * 2)
        b, full = tb(USE["bias"])
        pe.wait_ge(tb_free[b], full - 1)
        for w, col, n in ((rg_nat, 0, NG), (re_nat, NG, NE)):
            out = ps[0:1, TB0 + b, col:col + n]
            for kt in range(KT):
                pe.matmul(out, gb_nat[:, 1, kt:kt + 1], w[:, kt, :], start=(kt == 0), stop=False)
            last = pe.matmul(out, ones[0:1, 0:1], rbias[:, col:col + n], start=False, stop=True)
        last.then_inc(tb_full[b], 1)
        for i, (t0, m) in enumerate(TILES):
            pe.wait_ge(t_ready[i], 1)
            for q in range(4):
                b, full = tb(USE[f"r{i}{q}"])
                pe.wait_ge(tb_free[b], full - 1)
                for t in range(4):
                    last = pe.transpose(ps[:, TB0 + b, P * t:P * t + m], tok[0:m, i, 4 * q + t::KT],
                                        ident[0:m, 0:m])
                last.then_inc(tb_full[b], 1)
        pe.wait_ge(rw_ready, 2)
        pe.wait_ge(bias_ready, 1)
        wait_read(pe, "r22", "r23")
        b, full = tb(USE["lgT"])
        out = ps[0:NG + NE, TB0 + b, 0:NTOK]
        for kt in range(KT):
            pe.matmul(out, rw[:, kt, :], x1T[:, kt, :], start=(kt == 0), stop=False)
        for i, (t0, m) in enumerate(TILES):
            last = pe.matmul(out[:, t0:t0 + m], rbias_all[:, :], ones[0:1, 0:m], start=False, stop=(i == 2))
        last.then_inc(tb_full[b], 1)
        b, full = tb(USE["lg"])
        pe.wait_ge(lgT_ready, 1)
        pe.wait_ge(lgT_pad, 1)
        for i in range(3):
            last = pe.transpose(ps[:, TB0 + b, (NG + NE) * i:(NG + NE) * (i + 1)], lgT[:, P * i:P * (i + 1)],
                                ident[0:NG + NE, 0:NG + NE])
        last.then_inc(tb_full[b], 1)
        pe.wait_ge(mask_ready, 1)
        b, full = tb(USE["pos"])
        pe.wait_ge(tb_free[b], full - 1)
        for i, (t0, m) in enumerate(TILES):
            out = ps[:, TB0 + b, NE * i:NE * (i + 1)]
            for i2 in range(i):
                pe.matmul(out, ones[:, :], mask[:, i2, :], start=(i2 == 0), stop=False)
            last = pe.matmul(out, before[0:m, :], mask[0:m, i, :], start=(i == 0), stop=True)
        last.then_inc(tb_full[b], 1)
    GATE, UP, DOWN = 0, 1, 2
    HALF = (UP, GATE)

    def pe_experts(pe):
        def slots(n, e):
            pe.wait_ge(onehot_ready, n + 1)
            for i, (t0, m) in enumerate(TILES):
                fact = facts[0:m, i, e, :] if isinstance(e, int) else \
                    facts[0:m, i, bass.ds(e, 1), :].rearrange("p a b -> p (a b)")
                last = pe.matmul(ps[0:C, UP, 0:2], onehot[0:m, i, :], fact, start=(i == 0), stop=(i == 2))
            last.then_inc(slots_made, 1)

        def tokens(n, q):
            b, full = x_use(n, q)
            if q == 0:
                pe.wait_ge(gathered, 16 * n + 16)
            pe.wait_ge(tb_free[b], full - 1)
            for t in range(4):
                last = pe.transpose(ps[:, TB0 + b, C * t:C * (t + 1)], xg[0:C, 4 * q + t::KT],
                                    ident[0:C, 0:C])
            last.then_inc(tb_full[b], 1)

        def split_product(out, x, w, start, stop):
            pe.matmul(out, x[0], w[0], start=start, stop=False)
            pe.matmul(out, x[1], w[0], start=False, stop=False)
            return pe.matmul(out, x[0], w[1], start=False, stop=stop)

        def step(n, e, last_step):
            for m in range(HALVES):
                j, part = m // 2, m % 2
                pe.wait_ge(lo_ready, CHUNKS1 + m + 1 + n * HALVES)
                if j < 4:
                    b, full = x_use(n, j)
                    pe.wait_ge(tb_free[b], full)
                    wh = half(w_hi, m).rearrange("p (t f) -> p t f", t=2)
                    wl = half(w_lo, m).rearrange("p (t f) -> p t f", t=2)
                    for t in range(2):
                        kt = 4 * j + 2 * part + t
                        last = split_product(ps[0:C, GATE, :], (xgT_hi[:, kt, :], xgT_lo[:, kt, :]),
                                             (wh[:, t, :], wl[:, t, :]), kt == 0, kt == KT - 1)
                elif j < 8:
                    if m == 8 and not last_step:
                        pe.wait_ge(rows_ready, n + 2)
                    if m == 12:
                        pe.wait_ge(silu_ready, n + 1)
                    h = (j - 4) // 2
                    wh = half(w_hi, m).rearrange("p (t f) -> p t f", t=4)
                    wl = half(w_lo, m).rearrange("p (t f) -> p t f", t=4)
                    for t in range(4):
                        kt = 8 * (j % 2) + 4 * part + t
                        last = split_product(ps[0:C, HALF[h], 0:FH],
                                             (xgT_hi[:, kt, :], xgT_lo[:, kt, :]),
                                             (wh[:, t, :], wl[:, t, :]), kt == 0, kt == KT - 1)
                else:
                    f = j - 8
                    if m == 16:
                        pe.wait_ge(facts_ready, 1)
                        pe.wait_ge(y_read, n + 1)
                    if m in (16, 20):
                        pe.wait_ge(aT_lo_ready, 2 * n + f // 2 + 1)
                    for q in range(2):
                        col = slice(512 * q, 512 * (q + 1))
                        last = split_product(ps[0:C, DOWN + 2 * part + q, :], (aT_hi[:, f, :], aT_lo[:, f, :]),
                                             (half(w_hi, m)[:, col], half(w_lo, m)[:, col]),
                                             f == 0, f == FT - 1)
                last.then_inc(w_used, 1)
                if m == 5 and not last_step:
                    slots(n + 1, e + 1)
                if m in (13, 17):
                    h = (m - 13) // 4
                    pe.wait_ge(a_ready, 2 * n + h + 1)
                    for t in range(2):
                        f = 2 * h + t
                        last = pe.transpose(ps[:, HALF[h], C * t:C * (t + 1)], a_sb[0:C, P * f:P * (f + 1)],
                                            ident[0:C, 0:C])
                    last.then_inc(aT_full, 1)
                if m in (17, 19, 21, 23) and not last_step:
                    tokens(n + 1, (m - 17) // 2)

        def one_round(r):
            n = r * NE
            slots(n, 0)
            if isinstance(r, int):
                for i, (t0, m) in enumerate(TILES):
                    last = pe.matmul(ps[:, COUNTS, 0:NE], ones[0:m, :], mask[0:m, i, :],
                                     start=(i == 0), stop=(i == 2))
                last.then_inc(counted, 1)
            for q in range(4):
                tokens(n, q)
            each_expert(pe, r, step)

        each_round(pe, one_round)

    def act_router(act):
        act.wait_ge(norm_ready, 1)
        act.activation(tok[:, 1, :], tok[:, 1, :], ACT.Identity, bias=norm_bias[:, 1:2],
                       scale=vrstd[:, 1:2]).then_inc(t_ready[1], 1)
        b, full = tb(USE["bias"])
        act.wait_ge(tb_full[b], full)
        act.copy(rbias_all[:, :], ps[0:1, TB0 + b, 0:NG + NE]).then_inc(tb_free[b], 1)
        act.wait_ge(tb_free[b], full)
        act.sem_inc(bias_ready, 1)
        expert_hi(act, 0, 0)
        for i, (t0, m) in enumerate(TILES):
            for q in range(4):
                b, full = tb(USE[f"r{i}{q}"])
                act.wait_ge(tb_full[b], full)
                act.copy(x1T[:, 4 * q:4 * q + 4, t0:t0 + m],
                         ps[:, TB0 + b, :].rearrange("p (t c) -> p t c", t=4)[:, :, 0:m])\
                   .then_inc(tb_free[b], 1)
        for m in range(1, LEAD):
            expert_hi(act, 0, m)
        b, full = tb(USE["lgT"])
        act.wait_ge(tb_full[b], full)
        act.copy(lgT[:, 0:NTOK], ps[0:NG + NE, TB0 + b, 0:NTOK]).then_inc(tb_free[b], 1)
        act.wait_ge(tb_free[b], full)
        act.sem_inc(lgT_ready, 1)
        b, full = tb(USE["lg"])
        act.wait_ge(tb_full[b], full)
        act.copy(logits[:, :, :].rearrange("p i n -> p (i n)"), ps[:, TB0 + b, 0:3 * (NG + NE)])\
           .then_inc(tb_free[b], 1)
        act.wait_ge(tb_free[b], full)
        act.sem_inc(logits_ready, 1)
        act.wait_ge(gexp_in, 1)
        act.activation(expd[:, :, :], expd[:, :, :], ACT.Exp).then_inc(gexp_out, 1)
        act.wait_ge(x1_stored, 16 * 3)
        for i, (t0, m) in enumerate(TILES):
            act.mul(tok[0:m, i, :], tok[0:m, i, :], ALPHA).then_inc(alpha_ready, 1)

    def expert_hi(act, n, m):
        j, ahead = m // 2 % ECH, m // HALVES
        s, base_ = raw_slot(j)
        act.wait_ge(raw_full[s], 16 * (base_ + j // 6 + 1 + 2 * ahead) + n * 32)
        back = CHUNKS1 - RING + 1 + m // 2 if isinstance(n, int) and n == 0 and m < HRING else \
            CHUNKS1 + m + 1 - HRING
        act.wait_ge(w_used, back + n * HALVES)
        act.copy(half(w_hi, m), raw[s][:, HC * (m % 2):HC * (m % 2 + 1)]).then_inc(hi_ready, 1)

    def act_experts(act):
        act.sem_inc(y_read, 1)

        def tokens_hi(n, q):
            b, full = x_use(n, q)
            act.wait_ge(tb_full[b], full)
            act.copy(xgT_hi[:, 4 * q:4 * q + 4, :],
                           ps[:, TB0 + b, 0:4 * C].rearrange("p (t c) -> p t c", t=4))\
               .then_inc(xg_hi_ready, 1)

        def step(n, e, last_step):
            for m in range(LEAD, HALVES + (0 if last_step else LEAD)):
                expert_hi(act, n, m)
                if m == 9:
                    act.wait_ge(w_used, CHUNKS1 + 8 + n * HALVES)
                    act.activation(silu[0:C, :], ps[0:C, GATE, :], ACT.Silu).then_inc(silu_ready, 1)
                if m in (15, 19):
                    h = (m - 15) // 4
                    act.wait_ge(aT_full, 2 * n + h + 1)
                    act.copy(aT_hi[:, 2 * h:2 * h + 2, :],
                                   ps[:, HALF[h], 0:2 * C].rearrange("p (t c) -> p t c", t=2)).then_inc(aT_hi_ready, 1)
                if m in (19, 21, 23, 25) and not last_step:
                    tokens_hi(n + 1, (m - 19) // 2)
            act.wait_ge(w_used, CHUNKS1 + HALVES + n * HALVES)
            act.wait_ge(yout_free, n + 1)
            for q in range(2):
                last = act.copy(yout[0:C, 1024 * q:1024 * (q + 1)].rearrange("p (b c) -> p b c", b=2),
                                      ps[0:C, DOWN + 2 * q:DOWN + 2 * q + 2, :])
            last.then_inc(y_read, 1)

        def one_round(r):
            if not isinstance(r, int):
                for m in range(LEAD):
                    expert_hi(act, r * NE, m)
            for q in range(4):
                tokens_hi(r * NE, q)
            each_expert(act, r, step)

        each_round(act, one_round)

    def act_finish(act):
        for i in range(3):
            act.wait_ge(fin_var, i + 1)
            act.activation(vrstd[:, i:i + 1], vstd[:, i:i + 1], ACT.Sqrt).then_inc(fin_std, 1)
            if i < 2:
                act.wait_ge(fin_scale, i + 1)
                act.activation(tok[:, i, :], tok[:, i, :], ACT.Identity, bias=norm_bias[:, i:i + 1],
                               scale=vrstd[:, i:i + 1]).then_inc(fin_norm, 1)

    def dve_router(dve, steps, link):
        for i in (0, 2):
            m = TILES[i][1]
            dve.tensor_scalar(tok[0:m, i, :], tok[0:m, i, :], vmv[0:m, i, 0:1], vrstd[0:m, i:i + 1],
                              ALU.subtract, ALU.mult).then_inc(t_ready[i], 1)
        dve.wait_ge(gb_in, 64)
        expert_lo(dve, 0, 0)
        for i, (t0, m) in enumerate(TILES):
            dve.wait_ge(t_ready[i], 1)
            b, full = tb(USE[f"r{i}3"])
            dve.wait_ge(tb_full[b], full)
            dve.tensor_tensor(tok[0:m, i, :], tok[0:m, i, :], lng[0:m, :], ALU.mult)\
               .then_inc(xg_ready[i], 1)
        dve.wait_ge(xg_ready[1], 1)
        dve.tensor_tensor(tok[:, 1, :], tok[:, 1, :], lnb[:, :], ALU.add).then_inc(x1_ready[1], 1)
        for m in range(1, LEAD):
            expert_lo(dve, 0, m)

        def tt(out, a, b, op):
            link(dve.tensor_tensor(out, a, b, op))

        dve.wait_ge(logits_ready, 1)
        rows4 = logits[:, :, :].rearrange("p i (g j) -> p (i g) j", j=4)
        expd4 = expd[:, :, :].rearrange("p i (g j) -> p (i g) j", j=4)
        link(dve.tensor_reduce(most_of[:, :], rows4, AXX, ALU.max))
        dve.tensor_tensor(expd4, rows4, most_of[:, :].unsqueeze(2).to_broadcast([P, 3 * LG, 4]),
                          ALU.subtract).then_inc(gexp_in, 1)
        dve.wait_ge(pool_const, 14)
        SH = [P, 3 * LG, 4, 4]
        others, own = rows4.unsqueeze(2).to_broadcast(SH), rows4.unsqueeze(3).to_broadcast(SH)
        steps.inc(dve.tensor_tensor(beaten[:, :, :, 0:4], others, own, ALU.is_gt))
        tt(beaten[:, :, :, 4:8], others, own, ALU.is_equal)
        tt(beaten[:, :, :, 4:8], beaten[:, :, :, 4:8],
           earlier[:, :, :].unsqueeze(1).to_broadcast(SH), ALU.mult)
        link(dve.tensor_reduce(place_in[:, :, :].rearrange("p i (g j) -> p (i g) j", j=4),
                               beaten[:, :, :, :], AXX, ALU.add))
        link(dve.tensor_scalar(group_of[:, :, :], place_in[:, :, 0:NG], 0.0, None, ALU.is_equal))

        def by(t):
            return t.rearrange("p i (g j) -> p i g j", g=NG)

        in_group = group_of[:, :, :].unsqueeze(3).to_broadcast([P, 3, NG, EG])
        places = place_in[:, :, NG:NG + NE]
        dve.tensor_scalar(chosen[:, :, :], places, 2.0, None, ALU.is_lt).then_inc(chosen_ready, 1)
        dve.wait_ge(chosen_ready, 1)
        dve.tensor_tensor(by(mask[:, :, :]), by(chosen[:, :, :]), in_group, ALU.mult)\
           .then_inc(mask_ready, 1)
        dve.wait_ge(mask_ready, 1)
        dve.wait_ge(gexp_out, 1)
        steps.inc(dve.tensor_reduce(gsum[:, :], expd[:, :, 0:NG], AXX, ALU.add))
        tt(expd[:, :, NG:NG + NE], expd[:, :, NG:NG + NE], mask[:, :, :], ALU.mult)
        link(dve.tensor_reduce(esum[:, :], expd[:, :, NG:NG + NE], AXX, ALU.add))
        tt(esum[:, :], esum[:, :], gsum[:, :], ALU.mult)
        link(dve.reciprocal(esum[:, :], esum[:, :]))
        tt(facts[:, :, :, 1], expd[:, :, NG:NG + NE],
           esum[:, :].unsqueeze(2).to_broadcast([P, 3, NE]), ALU.mult)
        b, full = tb(USE["pos"])
        dve.wait_ge(tb_full[b], full)
        dve.scalar_tensor_tensor(
            out=rank[:, :, 0:NE], in0=ps[:, TB0 + b, 0:3 * NE].rearrange("p (i e) -> p i e", i=3),
            scalar=1.0, in1=mask[:, :, :], op0=ALU.add, op1=ALU.mult).then_inc(tb_free[b], 1)
        dve.wait_ge(tb_free[b], full)

    def dve_more_rounds(dve, steps, link):
        for r in range(1, ROUNDS):
            link(dve.tensor_scalar(rank[:, :, NE * r:NE * (r + 1)], rank[:, :, 0:NE],
                                   -float(C * r), None, ALU.add))
        dve.wait_ge(counted, 1)
        link(dve.tensor_reduce(count_max[:, :], ps[:, COUNTS, 0:NE], AXX, ALU.max))
        link(dve.tensor_copy(fullest[:, 0:1], count_max[:, :]))
        dve.sem_inc(facts_ready, 1)

    def expert_lo(dve, n, m):
        s, _ = raw_slot(m // 2 % ECH)
        dve.wait_ge(hi_ready, CHUNKS1 + m + 1 + n * HALVES)
        dve.tensor_tensor(half(w_lo, m), raw[s][:, HC * (m % 2):HC * (m % 2 + 1)],
                          half(w_hi, m).bitcast(FP32), ALU.subtract).then_inc(lo_ready, 1)

    def dve_experts(dve, steps, link):
        def place(n):
            dve.tensor_tensor(onehot[:, :, :], slots[:, 0:C].unsqueeze(1).to_broadcast([P, 3, C]),
                              rank[:, :, bass.ds(n, 1)].to_broadcast([P, 3, C]), ALU.is_equal)\
               .then_inc(onehot_ready, 1)

        def rows(n):
            dve.wait_ge(slots_made, n + 1)
            dve.tensor_scalar(gather_row[0:C, :], ps[0:C, UP, 0:1], BIG, None, ALU.add)
            dve.tensor_scalar(result_rows[0:C, bass.ds(n, 1)], ps[0:C, UP, 0:1], BIG, None, ALU.add)
            dve.tensor_copy(gates[0:C, bass.ds(n, 1)], ps[0:C, UP, 1:2]).then_inc(rows_ready, 1)

        def tokens_lo(n, q):
            b, full = x_use(n, q)
            dve.wait_ge(xg_hi_ready, 4 * n + q + 1)
            dve.tensor_tensor(xgT_lo[:, 4 * q:4 * q + 4, :],
                              ps[:, TB0 + b, 0:4 * C].rearrange("p (t c) -> p t c", t=4),
                              xgT_hi[:, 4 * q:4 * q + 4, :].bitcast(FP32), ALU.subtract)\
               .then_inc(tb_free[b], 1)

        def step(n, e, last_step):
            if not last_step:
                place(n + 1)
            for m in range(LEAD, HALVES + (0 if last_step else LEAD)):
                expert_lo(dve, n, m)
                if m == 7 and not last_step:
                    rows(n + 1)
                if m in (13, 17):
                    h = (m - 13) // 4
                    col = slice(FH * h, FH * (h + 1))
                    dve.wait_ge(w_used, CHUNKS1 + 12 + 4 * h + n * HALVES)
                    if h == 0:
                        dve.wait_ge(silu_ready, n + 1)
                        dve.wait_ge(rows_ready, n + 1)
                    dve.scalar_tensor_tensor(out=a_sb[0:C, col], in0=ps[0:C, HALF[h], 0:FH],
                                             scalar=gates[0:C, bass.ds(n, 1)], in1=silu[0:C, col],
                                             op0=ALU.mult, op1=ALU.mult).then_inc(a_ready, 1)
                if m in (15, 19):
                    h = (m - 15) // 4
                    dve.wait_ge(aT_hi_ready, 2 * n + h + 1)
                    dve.tensor_tensor(aT_lo[:, 2 * h:2 * h + 2, :],
                                      ps[:, HALF[h], 0:2 * C].rearrange("p (t c) -> p t c", t=2),
                                      aT_hi[:, 2 * h:2 * h + 2, :].bitcast(FP32), ALU.subtract)\
                       .then_inc(aT_lo_ready, 1)
                if m in (19, 21, 23, 25) and not last_step:
                    tokens_lo(n + 1, (m - 19) // 2)

        def one_round(r):
            n = r * NE
            place(n)
            rows(n)
            if isinstance(r, int):
                dve_more_rounds(dve, steps, link)
            if not isinstance(r, int):
                for m in range(LEAD):
                    expert_lo(dve, n, m)
            for q in range(4):
                tokens_lo(n, q)
            each_expert(dve, r, step)

        each_round(dve, one_round)

    def dve_finish(dve):
        steps = Tally(fin_step)

        def link(instruction):
            dve.wait_ge(fin_step, steps.inc(instruction))

        def statistics(i):
            m = TILES[i][1]
            for q in range(4):
                if q % 2 == 0:
                    dve.wait_ge(fin_in[i][q // 2], 16)
                steps.inc(dve.bn_stats(xstats[0:m, i, q, :], tok[0:m, i, 512 * q:512 * (q + 1)]))
            dve.wait_ge(fin_step, steps.value)
            link(dve.bn_aggr(vmv[0:m, i, :], xstats[0:m, i, 0:4, :].rearrange("p a b -> p (a b)")))
            dve.tensor_scalar(vstd[:, i:i + 1], vmv[:, i, 1:2], EPS, None, ALU.add).then_inc(fin_var, 1)

        def reciprocal(i):
            dve.wait_ge(fin_std, i + 1)
            link(dve.reciprocal(vrstd[:, i:i + 1], vrstd[:, i:i + 1]))

        for i in range(2):
            statistics(i)
            reciprocal(i)
            dve.scalar_tensor_tensor(out=norm_bias[:, i:i + 1], in0=vmv[:, i, 0:1], scalar=-1.0,
                                     in1=vrstd[:, i:i + 1], op0=ALU.mult, op1=ALU.mult)\
               .then_inc(fin_scale, 1)
        dve.wait_ge(ln2_in, 32)
        for i in range(2):
            dve.wait_ge(fin_norm, i + 1)
            dve.tensor_tensor(tok[:, i, :], tok[:, i, :], lng[:, :], ALU.mult).then_inc(fin_gain, 1)
        statistics(2)
        m = TILES[2][1]
        x = tok[0:m, 2, :]
        link(dve.scalar_tensor_tensor(out=x, in0=x, scalar=vmv[0:m, 2, 0:1], in1=lng[0:m, :],
                                      op0=ALU.subtract, op1=ALU.mult))
        reciprocal(2)
        dve.scalar_tensor_tensor(out=x, in0=x, scalar=vrstd[0:m, 2:3], in1=lnb[0:m, :],
                                 op0=ALU.mult, op1=ALU.add).then_inc(fin_ready[2], 1)

    with nc.Block() as block:
        @block.sync
        def _(sp):
            sp_program(sp)
            sp_experts(sp)
            sp_finish(sp)

        @block.gpsimd
        def _(pool):
            pool_program(pool)
            pool_experts(pool)
            pool_finish(pool)

        @block.scalar
        def _(act):
            act_mixer(act)
            act_router(act)
            act_experts(act)
            act_finish(act)

        @block.tensor
        def _(pe):
            pe_mixer(pe)
            pe_router(pe)
            pe_experts(pe)

        @block.vector
        def _(dve):
            steps, link = dve_mixer(dve)
            dve_router(dve, steps, link)
            dve_experts(dve, steps, link)
            dve_finish(dve)


_INS = ["x_prompt", "x_sample", "state_conv", "state_pool", "w_in", "conv_w", "sgu_ln_g", "sgu_ln_b",
        "sgu_w", "sgu_b", "pool_w", "pool_scale", "w_out", "ln1_g", "ln1_b", "router_group_w",
        "router_group_b", "router_expert_w", "router_expert_b", "expert_w_gate", "expert_w_up",
        "expert_w_down", "ln2_g", "ln2_b"]


def kernel(**inputs):
    import numpy as np
    import concourse.bacc as bacc
    from concourse import mybir as mb
    from concourse.bass_utils import run_bass_kernel_spmd

    nc = bacc.Bacc("TRN2", target_bir_lowering=False, num_devices=1)
    arrays, args = {}, []
    for name in _INS:
        a = np.ascontiguousarray(inputs[name])
        arrays[f"in_{name}"] = a
        args.append(nc.dram_tensor(f"in_{name}", a.shape, mb.dt.from_np(a.dtype),
                                   kind="ExternalInput").ap())
    b, s, d = inputs["x_prompt"].shape
    nb, nt = inputs["x_sample"].shape[0:2]
    depth, _, rows, conv = inputs["state_conv"].shape
    prows, pool = inputs["state_pool"].shape[2:4]
    chunk = inputs["sgu_ln_g"].shape[1]
    outs = [(b, s, d), (nb, nt, d), (depth, b, rows, conv), (depth, b, prows, pool),
            (depth, nb, rows, conv), (depth, nb, prows, pool), (depth, nb, nt, chunk)]
    for i, shape in enumerate(outs):
        args.append(nc.dram_tensor(f"out_{i}", shape, mb.dt.float32, kind="ExternalOutput").ap())
    hybrid_trunk_kernel(nc, *args)
    r = run_bass_kernel_spmd(nc, [arrays], core_ids=[0])
    return tuple(np.asarray(r.results[0][f"out_{i}"]).reshape(shape) for i, shape in enumerate(outs))
```
